# Optimizing a Trainium2 kernel written in Bass

```python
import jax, jax.numpy as jnp
from jax import lax
import numpy as np

D_MODEL = 1024
BATCH = 1
SEQ = 512
DEPTH = 1

CONV_WIDTH = D_MODEL
CONV_TAPS = 3
POOL_WIDTH = D_MODEL
POOL_WINDOWS = (2, 4, 8, 16)
N_POOL_GROUPS = len(POOL_WINDOWS)
POOL_GROUP = POOL_WIDTH // N_POOL_GROUPS
N_BRANCHES = 2
IN_COLS = 3 * CONV_WIDTH + POOL_WIDTH + N_BRANCHES * D_MODEL
PEER_HEADS = 8
N_KEYS = 128
N_EXPERTS = N_KEYS * N_KEYS
PEER_TOPK = 16
QUERY_DIM = 256
HALF_QUERY = QUERY_DIM // 2
TOKEN_CHUNK = 128
EPS = 1e-6

kernel_name = "hybrid_shortconv_pool_peer_block"

def rmsnorm(x, g):
    xf = x.astype(jnp.float32)
    y = xf * lax.rsqrt(jnp.mean(xf * xf, axis=-1, keepdims=True) + EPS)
    return (y * g.astype(jnp.float32)).astype(x.dtype)

def causal_short_conv(z, w):
    s = z.shape[1]
    zp = jnp.pad(z, ((0, 0), (CONV_TAPS - 1, 0), (0, 0)))
    y = w[0] * zp[:, 0:s]
    for k in range(1, CONV_TAPS):
        y = y + w[k] * zp[:, k:k + s]
    return y

def multiscale_causal_pool(p, w_grp, scale):
    b, s, _ = p.shape
    pf = p.astype(jnp.float32).reshape(b, s, N_POOL_GROUPS, POOL_GROUP)
    cs = jnp.cumsum(pf, axis=1)
    pos = jnp.arange(s)
    outs = []
    for g, win in enumerate(POOL_WINDOWS):
        c = cs[:, :, g]
        lag = jnp.pad(c, ((0, 0), (win, 0), (0, 0)))[:, :s]
        cnt = jnp.minimum(pos + 1, win).astype(jnp.float32)[None, :, None]
        outs.append((c - lag) / cnt - pf[:, :, g])
    pooled = jnp.stack(outs, axis=2).astype(p.dtype)
    mixed = jnp.einsum('bsgc,gcd->bsgd', pooled, w_grp)
    return mixed.reshape(b, s, POOL_WIDTH) * scale

def hybrid_mixer(xn, w_in, conv_w, w_conv_out, pool_w, pool_scale, w_pool_out, w_out):
    proj = xn @ w_in
    c0, c1, c2 = CONV_WIDTH, 2 * CONV_WIDTH, 3 * CONV_WIDTH
    c3 = c2 + POOL_WIDTH
    b_gate = proj[..., :c0]
    c_gate = proj[..., c0:c1]
    h = proj[..., c1:c2]
    p = proj[..., c2:c3]
    g_a = proj[..., c3:c3 + D_MODEL]
    g_b = proj[..., c3 + D_MODEL:]
    y_a = (b_gate * causal_short_conv(c_gate * h, conv_w)) @ w_conv_out
    y_b = multiscale_causal_pool(p, pool_w, pool_scale) @ w_pool_out
    merged = jax.nn.sigmoid(g_a) * y_a + jax.nn.sigmoid(g_b) * y_b
    return merged @ w_out

def peer(xn, w_query, sub_keys, expert_u, expert_v):
    b, s, d = xn.shape
    t = b * s
    xf = xn.reshape(t, d)
    q = (xf @ w_query).reshape(t, PEER_HEADS, 2, HALF_QUERY)
    scores = jnp.einsum('thpk,hpnk->thpn', q, sub_keys).astype(jnp.float32)
    v1, i1 = lax.top_k(scores[:, :, 0], PEER_TOPK)
    v2, i2 = lax.top_k(scores[:, :, 1], PEER_TOPK)
    cand = (v1[..., :, None] + v2[..., None, :]).reshape(t, PEER_HEADS, PEER_TOPK * PEER_TOPK)
    best, pos = lax.top_k(cand, PEER_TOPK)
    e1 = jnp.take_along_axis(i1, pos // PEER_TOPK, axis=-1)
    e2 = jnp.take_along_axis(i2, pos % PEER_TOPK, axis=-1)
    experts = (e1 * N_KEYS + e2).reshape(t, PEER_HEADS * PEER_TOPK)
    gates = jax.nn.softmax(best, axis=-1).reshape(t, PEER_HEADS * PEER_TOPK).astype(xn.dtype)

    def chunk_fn(args):
        xc, ic, gc = args
        u = expert_u[ic]
        a = jax.nn.gelu(jnp.einsum('cd,ced->ce', xc, u), approximate=False) * gc
        v = expert_v[ic]
        return jnp.einsum('ce,ced->cd', a, v)

    n_chunks = t // TOKEN_CHUNK
    out = lax.map(chunk_fn, (xf.reshape(n_chunks, TOKEN_CHUNK, d),
                             experts.reshape(n_chunks, TOKEN_CHUNK, -1),
                             gates.reshape(n_chunks, TOKEN_CHUNK, -1)))
    return out.reshape(b, s, d)

def setup_inputs(seed: int = 0) -> dict:
    key = jax.random.key(seed)
    ks = jax.random.split(key, 18)
    f32 = jnp.float32
    L, D = DEPTH, D_MODEL
    nrm = lambda k, shape, sc: (jax.random.normal(k, shape, f32) * sc)
    return {
        "x": jax.random.normal(ks[0], (BATCH, SEQ, D), f32),
        "norm_mix_g": 1.0 + nrm(ks[1], (L, D), 0.02),
        "w_in": nrm(ks[2], (L, D, IN_COLS), D ** -0.5),
        "conv_w": nrm(ks[3], (L, CONV_TAPS, CONV_WIDTH), CONV_TAPS ** -0.5),
        "w_conv_out": nrm(ks[4], (L, CONV_WIDTH, D), CONV_WIDTH ** -0.5),
        "pool_w": nrm(ks[5], (L, N_POOL_GROUPS, POOL_GROUP, POOL_GROUP), POOL_GROUP ** -0.5),
        "pool_scale": 1.0 + nrm(ks[6], (L, POOL_WIDTH), 0.02),
        "w_pool_out": nrm(ks[7], (L, POOL_WIDTH, D), POOL_WIDTH ** -0.5),
        "w_out": nrm(ks[8], (L, D, D), D ** -0.5),
        "norm_ffn_g": 1.0 + nrm(ks[9], (L, D), 0.02),
        "w_query": nrm(ks[10], (L, D, PEER_HEADS * QUERY_DIM), D ** -0.5),
        "sub_keys": nrm(ks[11], (L, PEER_HEADS, 2, N_KEYS, HALF_QUERY), HALF_QUERY ** -0.5),
        "expert_u": nrm(ks[12], (L, N_EXPERTS, D), D ** -0.5),
        "expert_v": nrm(ks[13], (L, N_EXPERTS, D), 0.5),
        "norm_final_g": 1.0 + nrm(ks[14], (D,), 0.02),
    }

def reference(x, norm_mix_g, w_in, conv_w, w_conv_out, pool_w, pool_scale, w_pool_out,
              w_out, norm_ffn_g, w_query, sub_keys, expert_u, expert_v, norm_final_g):
    h = x
    for l in range(DEPTH):
        xn = rmsnorm(h, norm_mix_g[l])
        h = h + hybrid_mixer(xn, w_in[l], conv_w[l], w_conv_out[l], pool_w[l],
                             pool_scale[l], w_pool_out[l], w_out[l])
        xn = rmsnorm(h, norm_ffn_g[l])
        h = h + peer(xn, w_query[l], sub_keys[l], expert_u[l], expert_v[l])
    return rmsnorm(h, norm_final_g)


_drawn_inputs = setup_inputs


def setup_inputs(seed=0):
    import zlib

    import numpy as np

    out = dict(_drawn_inputs(seed))
    spreads = {}
    factors = {}
    for name, (base, spread) in spreads.items():
        noise = np.random.default_rng([zlib.crc32(name.encode()), seed]).standard_normal(out[name].shape)
        drawn = base * np.exp(spread * noise) if base else spread * noise
        out[name] = __import__('jax').numpy.asarray(drawn.astype(out[name].dtype))
    for name, factor in factors.items():
        out[name] = (out[name] * factor).astype(out[name].dtype)
    return out
```

```python
from contextlib import ExitStack

import numpy as np

import concourse.bass as bass
import concourse.mybir as mybir

F32, F32R, U32 = mybir.dt.float32, mybir.dt.float32r, mybir.dt.uint32
ALU, ACT, AX = mybir.AluOpType, mybir.ActivationFunctionType, mybir.AxisListType

P = 128
T = 512
D = 1024
NB = D // P
TAPS = 3
WINDOWS = (2, 4, 8, 16)
PAD = max(WINDOWS)
HEADS = 8
TOPK = 16
KEYS = 128
HALVES = 2 * HEADS
CHUNKS = T // P
UNITS = CHUNKS * HEADS
EPS = 1e-6
SLOTS = 4
LOWEST = -3.4028234663852886e38

N_IN, N_POOL = 4 * NB, len(WINDOWS)
AT_POOL = N_IN
AT_GATE = AT_POOL + N_POOL
AT_OUT = AT_GATE + 4 * NB
AT_QUERY = AT_OUT + NB
AT_U = AT_QUERY + HALVES
AT_V = AT_U + KEYS
N_TILES = AT_V + KEYS

TOPK_STEPS = UNITS // 2
ONEHOT_AT = TOPK_STEPS + 2
TOKENS_PER_STEP = 64
ONEHOT_STEPS = T // TOKENS_PER_STEP
PLAIN_AT = ONEHOT_AT + ONEHOT_STEPS
U_STEPS = KEYS // SLOTS
TOKENS_PER_GROUP = 4
GROUPS_PER_STEP = TOKENS_PER_STEP // TOKENS_PER_GROUP
PIECE = 32
N_PIECES = T // PIECE

USES_GATE = NB
USES_OUT = USES_GATE + NB
USES_QUERY = USES_OUT + NB // SLOTS
USES_U = USES_QUERY + HALVES // SLOTS
USES_V = USES_U + U_STEPS

COL_G_MIX, COL_G_FFN, COL_G_FIN, COL_SCALE, COL_CONV = 0, 8, 16, 24, 32
COL_INV = COL_CONV + TAPS * NB
N_PARAMS = COL_INV + PAD


def ds(i, n=1):
    return bass.ds(i, n)


class MemoryMap:

    def __init__(self, nc, at):
        self.nc, self.at = nc, at

    def __call__(self, name, shape, dtype=F32):
        size = 4 * int(np.prod(shape[1:]))
        tensor = self.nc.alloc_sbuf_tensor_at(name, shape, dtype, offset=self.at)
        self.at += (size + 31) // 32 * 32
        return tensor


class Chain:

    def __init__(self, engine, sem):
        self.engine, self.sem, self.count, self.base = engine, sem, 0, 0

    def enter(self, i, per_pass):
        self.start, self.per_pass, self.count = self.base + self.count, per_pass, 0
        self.base = i * per_pass + self.start

    def leave(self, passes):
        assert self.count == self.per_pass, (self.count, self.per_pass)
        self.base, self.count = self.start + passes * self.per_pass, 0

    def did(self, instruction):
        instruction.then_inc(self.sem, 1)
        self.count += 1

    def wait(self):
        self.engine.wait_ge(self.sem, self.base + self.count)

    def hold(self, carrier):
        self.wait()
        self.engine.sem_inc(carrier, 1)


def build(nc, x_t, params_d, w_in_d, pool_d, gate_d, w_out_d, query_d, keys_d, u_d, v_d, out_d,
          act_dram, g_dram):
    ctx = ExitStack()
    with ctx:
        fixed = MemoryMap(nc, (nc.sbuf_base + 31) // 32 * 32)
        h_t = fixed("h_t", [P, NB, T])
        w_raw = fixed("w_raw", [P, SLOTS, D])
        w_hi = fixed("w_hi", [P, SLOTS, D], F32R)
        w_lo = fixed("w_lo", [P, SLOTS, D], F32R)
        xn_hi = fixed("xn_hi", [P, NB, T], F32R)
        xn_lo = fixed("xn_lo", [P, NB, T], F32R)
        scratch = fixed("scratch", [P, 2, T])
        row_stat = fixed("row_stat", [P, T])
        ones = fixed("ones", [P, P])
        ident = fixed("ident", [P, P])
        iota_key = fixed("iota_key", [P, KEYS])
        iota_rank = fixed("iota_rank", [P, TOPK], U32)
        params = fixed("params", [P, N_PARAMS])

        front = MemoryMap(nc, fixed.at)
        u_hi = front("u_hi", [P, NB, T], F32R)
        u_lo = front("u_lo", [P, NB, T], F32R)
        mix_hi = front("mix_hi", [P, NB, T], F32R)
        mix_lo = front("mix_lo", [P, NB, T], F32R)
        in_loop = MemoryMap(nc, front.at)
        c_sb = in_loop("c_sb", [P, T])
        z_pad = in_loop("z_pad", [P, TAPS - 1 + T])
        conv = in_loop("conv", [P, 2, T])
        u_f = in_loop("u_f", [P, T])
        p_pad = in_loop("p_pad", [P, PAD + T])
        sums = in_loop("sums", [P, 2, PAD + T])
        pool_f = in_loop("pool_f", [P, T])
        edge = in_loop("edge", [P, PAD])
        mixed_f = in_loop("mixed_f", [P, T])
        gate_loop = MemoryMap(nc, front.at)
        merged_hi = gate_loop("merged_hi", [P, NB, T], F32R)
        merged_lo = gate_loop("merged_lo", [P, NB, T], F32R)
        sig_a = gate_loop("sig_a", [P, T])
        sig_b = gate_loop("sig_b", [P, T])

        peer = MemoryMap(nc, fixed.at)
        keys_t = peer("keys_t", [P, HALVES, KEYS])
        q_sb = peer("q_sb", [P, SLOTS, T])
        scores = peer("scores", [P, CHUNKS, HALVES, KEYS])
        rest = MemoryMap(nc, peer.at)
        act_out = rest("act_out", [P, SLOTS, T])
        e1_t = rest("e1_t", [P, T])
        e2_t = rest("e2_t", [P, T])
        gate_t = rest("gate_t", [P, T])
        best = rest("best", [P, UNITS, TOPK])
        e1 = rest("e1", [P, UNITS, TOPK])
        e2 = rest("e2", [P, UNITS, TOPK])
        denom = rest("denom", [P, UNITS])
        top_v = rest("top_v", [P, 2, 2, TOPK])
        top_i = rest("top_i", [P, 2, 2, TOPK], U32)
        less = rest("less", [P, 4, KEYS])
        cand = rest("cand", [P, 2, TOPK * TOPK])
        cand_less = rest("cand_less", [P, 2, TOPK * TOPK])
        keyed = rest("keyed", [P, 4, KEYS])
        top_c = rest("top_c", [P, 2, TOPK])
        pos = rest("pos", [P, 2, TOPK], U32)
        rank = rest("rank", [P, 2, 2, TOPK], U32)
        found = rest("found", [P, 2, 2, TOPK, TOPK])
        assert rest.at <= nc.sbuf_usable_end and gate_loop.at <= nc.sbuf_usable_end
        g_build = MemoryMap(nc, fixed.at)
        oh1 = g_build("oh1", [P, SLOTS, TOKENS_PER_GROUP, KEYS])
        oh2 = g_build("oh2", [P, SLOTS, TOKENS_PER_GROUP, KEYS])
        g_sb = g_build("g_sb", [P, 2, KEYS, PIECE])
        assert g_build.at <= peer.at
        v_part = MemoryMap(nc, fixed.at)
        act_in = v_part("act_in", [P, SLOTS, T])
        g_in = v_part("g_in", [P, N_PIECES, SLOTS, PIECE])
        a_f = v_part("a_f", [P, 2, T])
        a_hi = v_part("a_hi", [P, SLOTS, T], F32R)
        a_lo = v_part("a_lo", [P, SLOTS, T], F32R)
        assert v_part.at <= peer.at
        out_sb = MemoryMap(nc, fixed.at)("out_sb", [P, NB, T])

        bank = [ctx.enter_context(nc.psum_tensor(f"bank{b}", [P, T], F32)) for b in range(8)]

        def sem(name):
            return ctx.enter_context(nc.semaphore(name))

        x_loaded = [sem(f"x_loaded{k}") for k in range(2)]
        params_loaded = sem("params_loaded")
        keys_loaded = sem("keys_loaded")
        raw_loaded = [sem(f"raw_loaded{k}") for k in range(SLOTS)]
        hi_done = sem("hi_done")
        lo_done = sem("lo_done")
        job_done = sem("job_done")
        bank_free = [sem(f"bank_free{b}") for b in range(SLOTS)]
        consts = sem("consts")
        squared = sem("squared")
        summed = sem("summed")
        h_ready = sem("h_ready")
        xn_f = sem("xn_f")
        xn_h = sem("xn_h")
        xn_l = sem("xn_l")
        c_copied, p_copied = sem("c_copied"), sem("p_copied")
        uf_ready, uh_ready, ul_ready = sem("uf_ready"), sem("uh_ready"), sem("ul_ready")
        pf_ready, ph_ready, pl_ready = sem("pf_ready"), sem("ph_ready"), sem("pl_ready")
        mf_ready, mh_ready, ml_ready = sem("mf_ready"), sem("mh_ready"), sem("ml_ready")
        sigmoids = sem("sigmoids")
        gf_ready, gh_ready, gl_ready = sem("gf_ready"), sem("gh_ready"), sem("gl_ready")
        q_ready, scored, scores_ready = sem("q_ready"), sem("scored"), sem("scores_ready")
        act_ready = sem("act_ready")
        act_stored = [sem(f"act_stored{b}") for b in range(SLOTS)]
        shifted, exp_ready, gates_ready = sem("shifted"), sem("exp_ready"), sem("gates_ready")
        turned, turned_copied = sem("turned"), sem("turned_copied")
        onehots_ready, onehots_used = sem("onehots_ready"), sem("onehots_used")
        g_copied = sem("g_copied")
        g_stored = [sem(f"g_stored{k}") for k in range(2)]
        act_loaded = [sem(f"act_loaded{b}") for b in range(SLOTS)]
        g_loaded = sem("g_loaded")
        af_ready, ah_ready, al_ready = sem("af_ready"), sem("ah_ready"), sem("al_ready")
        acc_done = sem("acc_done")
        h2_ready, out_ready, out_stored = sem("h2_ready"), sem("out_ready"), sem("out_stored")
        var_ready, root_ready = sem("var_ready"), sem("root_ready")
        held = sem("held")
        dve_step = sem("dve_step")

        block = ctx.enter_context(nc.Block())

        @block.sync
        def _(sp):
            def load_raw(source, k, n, slot):
                if not isinstance(n, int) or n >= SLOTS:
                    sp.wait_ge(lo_done, n - SLOTS + 1)
                sp.dma_start(w_raw[:, slot, :], source[ds(k), :, :].rearrange("o p d -> (o p) d")
                             ).then_inc(raw_loaded[slot], 16)

            def load_all(source, first, count, start=0):
                with sp.Fori(start // SLOTS, count // SLOTS) as i:
                    for b in range(SLOTS):
                        load_raw(source, SLOTS * i + b, SLOTS * i + (first + b), b)

            for half in range(2):
                sp.dma_start(h_t[:, 4 * half:4 * half + 4, :], x_t[:, 4 * half:4 * half + 4, :]
                             ).then_inc(x_loaded[half], 16)
            sp.dma_start(params[:], params_d).then_inc(params_loaded, 16)
            for b in range(SLOTS):
                load_raw(w_in_d, b, b, b)
            load_all(w_in_d, 0, N_IN, start=SLOTS)
            load_all(pool_d, AT_POOL, N_POOL)
            load_all(gate_d, AT_GATE, 4 * NB)
            load_all(w_out_d, AT_OUT, NB)
            for k in range(HALVES):
                if k == 2 * SLOTS:
                    sp.wait_ge(job_done, AT_QUERY)
                    sp.dma_start(keys_t[:], keys_d).then_inc(keys_loaded, 16)
                load_raw(query_d, k, AT_QUERY + k, k % SLOTS)
            load_all(u_d, AT_U, KEYS)

            for k in range(2):
                sp.wait_ge(g_stored[k], 16 * N_PIECES // 2)

            def load_v_group(g):
                for b in range(SLOTS):
                    load_raw(v_d, SLOTS * g + b, SLOTS * g + (AT_V + b), b)
                    if not isinstance(g, int):
                        sp.wait_ge(af_ready, SLOTS * g + (b - SLOTS + 1))
                    sp.wait_ge(act_stored[b], 16 * g + 16)
                    sp.dma_start(act_in[:, b, :], act_dram[ds(SLOTS * g + b), :, :].rearrange("o p t -> (o p) t")
                                 ).then_inc(act_loaded[b], 16)
                    if b == 0:
                        if not isinstance(g, int):
                            sp.wait_ge(af_ready, SLOTS * g)
                        sp.dma_start(g_in[:], g_dram[:, :, ds(SLOTS * g, SLOTS), :]).then_inc(g_loaded, 16)

            load_v_group(0)
            with sp.Fori(1, KEYS // SLOTS) as g:
                load_v_group(g)

            for j in range(NB):
                sp.wait_ge(out_ready, j + 1)
                sp.dma_start(out_d[:, j, :], out_sb[:, j, :]).then_inc(out_stored, 16)
            sp.wait_ge(out_stored, 16 * NB)

        @block.gpsimd
        def _(pool):
            pool.memset(ones[:], 1.0).then_inc(consts, 1)
            pool.memset(z_pad[:, 0:TAPS - 1], 0.0).then_inc(consts, 1)
            pool.memset(p_pad[:, 0:PAD], 0.0).then_inc(consts, 1)
            pool.memset(ident[:], 0.0).then_inc(consts, 1)
            pool.iota(iota_rank[:], pattern=[[1, TOPK]], base=0, channel_multiplier=0).then_inc(consts, 1)
            pool.iota(iota_key[:], pattern=[[1, KEYS]], base=0, channel_multiplier=0,
                      allow_small_or_imprecise_dtypes=True).then_inc(consts, 1)
            pool.wait_ge(consts, 6)
            pool.affine_select(out=ident[:], in_=ident[:], compare_op=ALU.not_equal, fill=1.0, base=0,
                               pattern=[[-1, P]], channel_multiplier=1).then_inc(consts, 1)

            def store_activations(step):
                for b in range(SLOTS):
                    pool.wait_ge(act_ready, SLOTS * step + (b + 1))
                    pool.dma_start(act_dram[ds(SLOTS * step + b), :, :].rearrange("o p t -> (o p) t"),
                                   act_out[:, b, :]).then_inc(act_stored[b], 16)

            with pool.Fori(0, ONEHOT_AT) as step:
                store_activations(step)
            with pool.Fori(0, ONEHOT_STEPS) as s:
                store_activations(s + ONEHOT_AT)
                for k in range(2):
                    pool.wait_ge(g_copied, GROUPS_PER_STEP * s + (SLOTS + GROUPS_PER_STEP // 2 * (k + 1)))
                    pool.dma_start(g_dram[:, ds(2 * s + k), :, :].rearrange("p o e t -> p (o e) t"),
                                   g_sb[:, k, :, :]).then_inc(g_stored[k], 16)
            with pool.Fori(PLAIN_AT, U_STEPS) as step:
                store_activations(step)

        @block.scalar
        def _(act):
            def root(count):
                act.wait_ge(var_ready, count)
                act.activation(scratch[:, 0, :], row_stat[:], ACT.Sqrt).then_inc(root_ready, 1)

            def split_weight(n, slot, times):
                act.wait_ge(raw_loaded[slot], 16 * times)
                if not isinstance(n, int) or n >= SLOTS:
                    act.wait_ge(job_done, n - SLOTS + 1)
                act.activation(w_hi[:, slot, :], w_raw[:, slot, :], ACT.Copy).then_inc(hi_done, 1)

            def norm_hi(base):
                for j in range(NB):
                    act.wait_ge(xn_f, base + j + 1)
                    act.activation(xn_hi[:, j, :], scratch[:, j % 2, :], ACT.Copy).then_inc(xn_h, 1)

            for j in range(NB):
                if j % 4 == 0:
                    act.wait_ge(x_loaded[j // 4], 16)
                if j >= 2:
                    act.wait_ge(summed, j - 1)
                act.activation(scratch[:, j % 2, :], h_t[:, j, :], ACT.Square).then_inc(squared, 1)
            split_weight(0, 0, 1)
            root(1)
            split_weight(1, 1, 1)
            norm_hi(0)
            split_weight(2, 2, 1)
            split_weight(3, 3, 1)

            with act.Fori(0, NB) as i:
                act.wait_ge(job_done, SLOTS * i + 1)
                act.activation(c_sb[:], bank[0][:], ACT.Copy).then_inc(c_copied, 1)
                split_weight(SLOTS * i + 4, 0, i + 2)
                split_weight(SLOTS * i + 5, 1, i + 2)
                split_weight(SLOTS * i + 6, 2, i + 2)
                act.wait_ge(uf_ready, i + 1)
                act.activation(u_hi[:, ds(i), :], u_f[:], ACT.Copy).then_inc(uh_ready, 1)
                act.wait_ge(job_done, SLOTS * i + 4)
                act.activation(p_pad[:, PAD:], bank[3][:], ACT.Copy).then_inc(p_copied, 1)
                split_weight(SLOTS * i + 7, 3, i + 2)
                act.wait_ge(pf_ready, i + 1)
                act.activation(mix_hi[:, ds(i), :], pool_f[:], ACT.Copy).then_inc(ph_ready, 1)

            for g in range(N_POOL):
                act.wait_ge(job_done, AT_POOL + g + 1)
                for jo in range(2):
                    j = 2 * g + jo
                    if j >= 1:
                        act.wait_ge(ml_ready, j)
                    act.activation(mixed_f[:], bank[4 + 2 * (g % 2) + jo][:], ACT.Copy,
                                   scale=params[:, COL_SCALE + j:COL_SCALE + j + 1]).then_inc(mf_ready, 1)
                    act.wait_ge(mf_ready, j + 1)
                    act.activation(mix_hi[:, j, :], mixed_f[:], ACT.Copy).then_inc(mh_ready, 1)
                split_weight(AT_GATE + g, g, NB + 2)

            with act.Fori(0, NB) as i:
                for b, sig in ((0, sig_a), (1, sig_b)):
                    act.wait_ge(job_done, SLOTS * i + (AT_GATE + b + 1))
                    act.activation(sig[:], bank[b][:], ACT.Sigmoid).then_inc(sigmoids, 1)
                    split_weight(SLOTS * i + (AT_GATE + SLOTS + b), b, i + (NB + 3))
                for b in (2, 3):
                    split_weight(SLOTS * i + (AT_GATE + SLOTS + b), b, i + (NB + 3))
                act.wait_ge(gf_ready, i + 1)
                act.activation(merged_hi[:, ds(i), :], scratch[:, 0, :], ACT.Copy).then_inc(gh_ready, 1)

            with act.Fori(0, NB // SLOTS) as i:
                for b in range(SLOTS):
                    split_weight(SLOTS * i + (AT_OUT + SLOTS + b), b, i + (2 * NB + 3))
                    act.wait_ge(h_ready, SLOTS * i + (b + 1))
                    act.activation(scratch[:, b % 2, :], h_t[:, ds(SLOTS * i + b), :], ACT.Square).then_inc(squared, 1)
            root(2)
            norm_hi(NB)

            with act.Fori(0, HALVES // SLOTS) as i:
                def copy_scores(b):
                    act.wait_ge(scored, SLOTS * i + (b + 1))
                    act.activation(scores[:, :, ds(SLOTS * i + b), :].rearrange("p c o n -> p c (o n)"),
                                   bank[4 + b][:].rearrange("p (c n) -> p c n", c=CHUNKS),
                                   ACT.Copy).then_inc(scores_ready, 1)

                for b in range(SLOTS):
                    act.wait_ge(job_done, SLOTS * i + (AT_QUERY + b + 1))
                    act.activation(q_sb[:, b, :], bank[b][:], ACT.Copy).then_inc(q_ready, 1)
                    split_weight(SLOTS * i + (AT_QUERY + SLOTS + b), b, i + (AT_QUERY // SLOTS + 2))
                    if b >= 1:
                        copy_scores(b - 1)
                copy_scores(SLOTS - 1)

            def gelu_tile(step, b):
                act.wait_ge(job_done, SLOTS * step + (AT_U + b + 1))
                if not isinstance(step, int) or step > 0:
                    act.wait_ge(act_stored[b], 16 * step)
                act.activation(act_out[:, b, :], bank[b][:], ACT.Gelu).then_inc(act_ready, 1)
                split_weight(SLOTS * step + (AT_U + SLOTS + b), b, step + (AT_U // SLOTS + 2))

            def copy_g(s, q):
                if q % 8 == 0 and not isinstance(s, int):
                    act.wait_ge(g_stored[q // 8], 16 * s)
                act.wait_ge(onehots_used, GROUPS_PER_STEP * s + (SLOTS + q + 1))
                t = TOKENS_PER_GROUP * (q % 8)
                act.activation(g_sb[:, q // 8, :, t:t + TOKENS_PER_GROUP].rearrange("p e t -> p t e"),
                               bank[4 + q % SLOTS][:].rearrange("p (t e) -> p t e", e=KEYS),
                               ACT.Copy).then_inc(g_copied, 1)

            def g_step(s):
                for b in range(SLOTS):
                    gelu_tile(s + ONEHOT_AT, b)
                    for q in range(4 * b, 4 * b + 4):
                        copy_g(s, q)

            for b in range(SLOTS):
                gelu_tile(0, b)
            with act.Fori(1, TOPK_STEPS + 1) as step:
                for b in range(SLOTS):
                    gelu_tile(step, b)
            act.wait_ge(shifted, 1)
            act.activation(best[:], best[:], ACT.Exp).then_inc(exp_ready, 1)
            for b in range(SLOTS):
                gelu_tile(TOPK_STEPS + 1, b)
            for k, turned_to in enumerate((e1_t, e2_t, gate_t)):
                act.wait_ge(turned, k + 1)
                act.activation(turned_to[:], bank[4 + k][:], ACT.Copy).then_inc(turned_copied, 1)
            act.sem_inc(g_copied, SLOTS)
            g_step(0)
            with act.Fori(1, ONEHOT_STEPS) as s:
                g_step(s)
            with act.Fori(PLAIN_AT, U_STEPS - 1) as step:
                for b in range(SLOTS):
                    gelu_tile(step, b)

            def split_a(m, b):
                act.wait_ge(af_ready, m + 1)
                act.activation(a_hi[:, b, :], a_f[:, b % 2, :], ACT.Copy).then_inc(ah_ready, 1)

            for b in range(SLOTS):
                gelu_tile(U_STEPS - 1, b)
                split_a(b, b)
            with act.Fori(1, KEYS // SLOTS) as g:
                for b in range(SLOTS):
                    split_weight(SLOTS * g + (AT_V + b), b, g + (AT_V // SLOTS + 1))
                    split_a(SLOTS * g + b, b)

            for j in range(NB):
                act.wait_ge(h2_ready, j + 1)
                if j >= 2:
                    act.wait_ge(summed, NB + 1 + j - 1)
                act.activation(scratch[:, j % 2, :], h_t[:, j, :], ACT.Square).then_inc(squared, 1)
            root(3)

        @block.tensor
        def _(pe):
            def k_block(tensor, slot, k):
                return tensor[:, slot, k * P:(k + 1) * P]

            def tile_product(n, b, uses, act_hi, act_lo):
                pe.wait_ge(lo_done, n + 1)
                pe.wait_ge(bank_free[b], uses)
                for k in range(NB):
                    hi, lo = k_block(w_hi, b, k), k_block(w_lo, b, k)
                    pe.matmul(bank[b][:], hi, act_hi[:, k, :], start=k == 0, stop=False)
                    pe.matmul(bank[b][:], hi, act_lo[:, k, :], start=False, stop=False)
                    last = pe.matmul(bank[b][:], lo, act_hi[:, k, :], start=False, stop=k == NB - 1)
                last.then_inc(job_done, 1)

            pe.wait_ge(consts, 7)
            for j in range(NB):
                pe.wait_ge(squared, j + 1)
                pe.matmul(bank[4][:], ones[:], scratch[:, j % 2, :], start=j == 0, stop=j == NB - 1
                          ).then_inc(summed, 1)

            pe.wait_ge(xn_l, NB)
            with pe.Fori(0, NB) as i:
                for b in range(SLOTS):
                    tile_product(SLOTS * i + b, b, i + 1, xn_hi, xn_lo)

            pe.wait_ge(pl_ready, NB)
            for g in range(N_POOL):
                pe.wait_ge(lo_done, AT_POOL + g + 1)
                if g >= 2:
                    pe.wait_ge(mf_ready, 2 * (g - 1))
                for jo in range(2):
                    to = bank[4 + 2 * (g % 2) + jo]
                    for ki in range(2):
                        hi, lo = k_block(w_hi, g, 2 * ki + jo), k_block(w_lo, g, 2 * ki + jo)
                        x_hi, x_lo = mix_hi[:, 2 * g + ki, :], mix_lo[:, 2 * g + ki, :]
                        pe.matmul(to[:], hi, x_hi, start=ki == 0, stop=False)
                        pe.matmul(to[:], hi, x_lo, start=False, stop=False)
                        last = pe.matmul(to[:], lo, x_hi, start=False, stop=ki == 1)
                last.then_inc(job_done, 1)

            with pe.Fori(0, NB) as i:
                for b, (a_h, a_l) in enumerate(((xn_hi, xn_lo), (xn_hi, xn_lo), (u_hi, u_lo), (mix_hi, mix_lo))):
                    if b == 2:
                        pe.wait_ge(ul_ready, NB)
                        pe.wait_ge(ml_ready, NB)
                    tile_product(SLOTS * i + (AT_GATE + b), b, i + (USES_GATE + 1), a_h, a_l)

            pe.wait_ge(gl_ready, NB)
            with pe.Fori(0, NB // SLOTS) as i:
                for b in range(SLOTS):
                    tile_product(SLOTS * i + (AT_OUT + b), b, i + (USES_OUT + 1), merged_hi, merged_lo)
            pe.wait_ge(h_ready, NB + 1)
            pe.matmul(bank[4][:], ones[:], row_stat[:], start=True, stop=True).then_inc(summed, 1)

            pe.wait_ge(xn_l, 2 * NB)
            pe.wait_ge(keys_loaded, 16)
            with pe.Fori(0, HALVES // SLOTS) as i:
                def score(b):
                    pe.wait_ge(q_ready, SLOTS * i + (b + 1))
                    for c in range(CHUNKS):
                        last = pe.matmul(bank[4 + b][:, c * KEYS:(c + 1) * KEYS], q_sb[:, b, c * P:(c + 1) * P],
                                         keys_t[:, ds(SLOTS * i + b), :].rearrange("p o n -> p (o n)"),
                                         start=True, stop=True)
                    last.then_inc(scored, 1)

                for b in range(SLOTS):
                    tile_product(SLOTS * i + (AT_QUERY + b), b, i + (USES_QUERY + 1), xn_hi, xn_lo)
                    if b >= 1:
                        score(b - 1)
                score(SLOTS - 1)

            def u_tile(step, b):
                tile_product(SLOTS * step + (AT_U + b), b, step + (USES_U + 1), xn_hi, xn_lo)

            with pe.Fori(0, ONEHOT_AT) as step:
                for b in range(SLOTS):
                    u_tile(step, b)

            pe.wait_ge(scores_ready, HALVES)
            pe.wait_ge(gates_ready, 1)
            for k, tensor in enumerate((e1, e2, best)):
                for c in range(CHUNKS):
                    last = pe.transpose(bank[4 + k][:, c * P:(c + 1) * P],
                                        tensor[:, c * HEADS:(c + 1) * HEADS, :].rearrange("p u r -> p (u r)"),
                                        ident[:])
                last.then_inc(turned, 1)

            pe.sem_inc(onehots_used, SLOTS)
            with pe.Fori(0, ONEHOT_STEPS) as s:
                for b in range(SLOTS):
                    u_tile(s + ONEHOT_AT, b)
                    for q in range(4 * b, 4 * b + 4):
                        pe.wait_ge(onehots_ready, GROUPS_PER_STEP * s + (q + 1))
                        pe.wait_ge(g_copied, GROUPS_PER_STEP * s + (q + 1))
                        for t in range(TOKENS_PER_GROUP):
                            last = pe.matmul(bank[4 + q % SLOTS][:, t * KEYS:(t + 1) * KEYS],
                                             oh1[:, q % SLOTS, t, :], oh2[:, q % SLOTS, t, :],
                                             start=True, stop=True)
                        last.then_inc(onehots_used, 1)
            with pe.Fori(PLAIN_AT, U_STEPS) as step:
                for b in range(SLOTS):
                    u_tile(step, b)

            def v_tile(g, b, first=False, final=False):
                pe.wait_ge(lo_done, SLOTS * g + (AT_V + b + 1))
                pe.wait_ge(al_ready, SLOTS * g + (b + 1))
                for j in range(NB):
                    if first and j < SLOTS:
                        pe.wait_ge(bank_free[j], USES_V + 1)
                    hi, lo = k_block(w_hi, b, j), k_block(w_lo, b, j)
                    pe.matmul(bank[j][:], hi, a_hi[:, b, :], start=first, stop=False)
                    pe.matmul(bank[j][:], hi, a_lo[:, b, :], start=False, stop=False)
                    last = pe.matmul(bank[j][:], lo, a_hi[:, b, :], start=False, stop=final)
                    if final:
                        last.then_inc(acc_done, 1)
                if not final:
                    last.then_inc(job_done, 1)

            pe.wait_ge(g_copied, SLOTS + T // TOKENS_PER_GROUP)
            for b in range(SLOTS):
                v_tile(0, b, first=b == 0)
            with pe.Fori(1, KEYS // SLOTS - 1) as g:
                for b in range(SLOTS):
                    v_tile(g, b)
            for b in range(SLOTS):
                v_tile(KEYS // SLOTS - 1, b, final=b == SLOTS - 1)

            for j in range(NB):
                pe.wait_ge(squared, 2 * NB + j + 1)
                pe.matmul(bank[0][:], ones[:], scratch[:, j % 2, :], start=j == 0, stop=j == NB - 1
                          ).then_inc(summed, 1)

        @block.vector
        def _(dve):
            chain = Chain(dve, dve_step)
            norms = [0]

            def split_weight(n, slot):
                dve.wait_ge(hi_done, n + 1)
                dve.tensor_tensor(w_lo[:, slot, :], w_raw[:, slot, :], w_hi[:, slot, :].bitcast(F32),
                                  ALU.subtract).then_inc(lo_done, 1)

            def inverse_rms(source):
                dve.tensor_scalar(row_stat[:], source, 1.0 / D, EPS, ALU.mult, ALU.add).then_inc(var_ready, 1)
                norms[0] += 1
                dve.wait_ge(root_ready, norms[0])
                y, t = scratch[:, 1, :], scratch[:, 0, :]
                chain.did(dve.reciprocal(y, t))
                chain.wait()
                chain.did(dve.tensor_tensor(t, y, y, ALU.mult))
                chain.wait()
                chain.did(dve.tensor_tensor(t, t, row_stat[:], ALU.mult))
                chain.wait()
                chain.did(dve.tensor_scalar(t, t, -0.5, 1.5, ALU.mult, ALU.add))
                chain.wait()
                chain.did(dve.tensor_tensor(row_stat[:], y, t, ALU.mult))
                chain.wait()

            def norm_apply(base, gain_col):
                def lo(j):
                    dve.wait_ge(xn_h, base + j + 1)
                    dve.tensor_tensor(xn_lo[:, j, :], scratch[:, j % 2, :], xn_hi[:, j, :].bitcast(F32),
                                      ALU.subtract).then_inc(xn_l, 1)

                for j in range(NB):
                    if j >= 2:
                        dve.wait_ge(xn_l, base + j - 1)
                    dve.scalar_tensor_tensor(scratch[:, j % 2, :], h_t[:, j, :],
                                             params[:, gain_col + j:gain_col + j + 1], row_stat[:],
                                             ALU.mult, ALU.mult).then_inc(xn_f, 1)
                    if j >= 1:
                        lo(j - 1)
                lo(NB - 1)

            for b in range(SLOTS):
                dve.sem_inc(bank_free[b], 1)
            dve.wait_ge(params_loaded, 16)
            dve.wait_ge(summed, NB)
            inverse_rms(bank[4][:])
            split_weight(0, 0)
            norm_apply(0, COL_G_MIX)
            for b in range(1, SLOTS):
                split_weight(b, b)
            dve.wait_ge(consts, 7)

            def in_block(i, window):
                tap = lambda k: params[:, ds(TAPS * i + (COL_CONV + k))]
                dve.wait_ge(c_copied, i + 1)
                dve.sem_inc(bank_free[0], 1)
                dve.wait_ge(job_done, SLOTS * i + 2)
                chain.did(dve.tensor_tensor(z_pad[:, TAPS - 1:], bank[1][:], c_sb[:], ALU.mult))
                split_weight(SLOTS * i + 4, 0)
                chain.wait()
                dve.sem_inc(bank_free[1], 1)
                chain.did(dve.tensor_scalar(conv[:, 0, :], z_pad[:, 0:T], tap(0), None, ALU.mult))
                chain.wait()
                chain.did(dve.scalar_tensor_tensor(conv[:, 1, :], z_pad[:, 1:1 + T], tap(1), conv[:, 0, :],
                                                   ALU.mult, ALU.add))
                chain.wait()
                chain.did(dve.scalar_tensor_tensor(conv[:, 0, :], z_pad[:, 2:2 + T], tap(2), conv[:, 1, :],
                                                   ALU.mult, ALU.add))
                split_weight(SLOTS * i + 5, 1)
                dve.wait_ge(job_done, SLOTS * i + 3)
                chain.wait()
                dve.tensor_tensor(u_f[:], bank[2][:], conv[:, 0, :], ALU.mult).then_inc(uf_ready, 1)
                split_weight(SLOTS * i + 6, 2)
                dve.wait_ge(uh_ready, i + 1)
                dve.sem_inc(bank_free[2], 1)
                dve.tensor_tensor(u_lo[:, ds(i), :], u_f[:], u_hi[:, ds(i), :].bitcast(F32), ALU.subtract
                                  ).then_inc(ul_ready, 1)
                dve.wait_ge(p_copied, i + 1)
                dve.sem_inc(bank_free[3], 1)
                source, width, side = p_pad[:], 1, 0
                while width < window:
                    begin = 2 * width - 1
                    chain.did(dve.tensor_tensor(sums[:, side, begin:], source[:, begin:],
                                                source[:, begin - width:PAD + T - width], ALU.add))
                    chain.wait()
                    source, width, side = sums[:, side, :], 2 * width, 1 - side
                chain.did(dve.tensor_tensor(edge[:, 0:window], source[:, PAD:PAD + window],
                                            params[:, COL_INV:COL_INV + window], ALU.mult))
                chain.did(dve.scalar_tensor_tensor(pool_f[:], source[:, PAD:], 1.0 / window, p_pad[:, PAD:],
                                                   ALU.mult, ALU.subtract))
                chain.wait()
                dve.tensor_tensor(pool_f[:, 0:window], edge[:, 0:window], p_pad[:, PAD:PAD + window],
                                  ALU.subtract).then_inc(pf_ready, 1)
                split_weight(SLOTS * i + 7, 3)
                dve.wait_ge(ph_ready, i + 1)
                dve.tensor_tensor(mix_lo[:, ds(i), :], pool_f[:], mix_hi[:, ds(i), :].bitcast(F32),
                                  ALU.subtract).then_inc(pl_ready, 1)

            for g, window in enumerate(WINDOWS):
                with dve.Fori(2 * g, 2 * g + 2) as i:
                    chain.enter(i - 2 * g, 4 + (window.bit_length() - 1) + 2)
                    in_block(i, window)
                chain.leave(2)

            for g in range(N_POOL):
                for jo in range(2):
                    j = 2 * g + jo
                    dve.wait_ge(mh_ready, j + 1)
                    dve.tensor_tensor(mix_lo[:, j, :], mixed_f[:], mix_hi[:, j, :].bitcast(F32), ALU.subtract
                                      ).then_inc(ml_ready, 1)
                split_weight(AT_GATE + g, g)

            with dve.Fori(0, NB) as i:
                chain.enter(i, 2)
                for b in range(2):
                    dve.wait_ge(sigmoids, 2 * i + (b + 1))
                    dve.sem_inc(bank_free[b], 1)
                    split_weight(SLOTS * i + (AT_GATE + SLOTS + b), b)
                for b, sig in ((2, sig_a), (3, sig_b)):
                    dve.wait_ge(job_done, SLOTS * i + (AT_GATE + b + 1))
                    chain.did(dve.tensor_tensor(sig[:], bank[b][:], sig[:], ALU.mult))
                    split_weight(SLOTS * i + (AT_GATE + SLOTS + b), b)
                    chain.wait()
                    dve.sem_inc(bank_free[b], 1)
                dve.tensor_tensor(scratch[:, 0, :], sig_a[:], sig_b[:], ALU.add).then_inc(gf_ready, 1)
                dve.wait_ge(gh_ready, i + 1)
                dve.tensor_tensor(merged_lo[:, ds(i), :], scratch[:, 0, :], merged_hi[:, ds(i), :].bitcast(F32),
                                  ALU.subtract).then_inc(gl_ready, 1)
            chain.leave(NB)

            chain.did(dve.memset(row_stat[:], 0.0))
            with dve.Fori(0, NB // SLOTS) as i:
                chain.enter(i, SLOTS)
                for b in range(SLOTS):
                    block_j = h_t[:, ds(SLOTS * i + b), :].rearrange("p o t -> p (o t)")
                    dve.wait_ge(job_done, SLOTS * i + (AT_OUT + b + 1))
                    dve.tensor_tensor(block_j, bank[b][:], block_j, ALU.add).then_inc(h_ready, 1)
                    split_weight(SLOTS * i + (AT_OUT + SLOTS + b), b)
                    dve.wait_ge(squared, SLOTS * i + (NB + b + 1))
                    dve.sem_inc(bank_free[b], 1)
                    chain.wait()
                    chain.did(dve.tensor_tensor(row_stat[:], row_stat[:], scratch[:, b % 2, :], ALU.add))
            chain.leave(NB // SLOTS)
            chain.wait()
            dve.sem_inc(h_ready, 1)
            dve.wait_ge(summed, NB + 1)
            inverse_rms(bank[4][:])
            norm_apply(NB, COL_G_FFN)

            with dve.Fori(0, HALVES // SLOTS) as i:
                for b in range(SLOTS):
                    dve.wait_ge(q_ready, SLOTS * i + (b + 1))
                    dve.sem_inc(bank_free[b], 1)
                    split_weight(SLOTS * i + (AT_QUERY + SLOTS + b), b)

            def u_split(step, b):
                dve.wait_ge(act_ready, SLOTS * step + (b + 1))
                dve.sem_inc(bank_free[b], 1)
                split_weight(SLOTS * step + (AT_U + SLOTS + b), b)

            def retrieve(i, split):
                table = scores[:].rearrange("p c q n -> p (c q) n")
                halves = [(k, k // 2, k % 2) for k in range(4)]
                row = lambda k: keyed[:, k, :]
                chain.did(dve.tensor_copy(keyed[:], table[:, ds(4 * i, 4), :]))
                chain.hold(held)
                for k, u, h in halves:
                    chain.did(dve.max(top_v[:, u, h, 0:8], row(k)))
                chain.hold(held)
                for k, u, h in halves:
                    chain.did(dve.max_index(top_i[:, u, h, 0:8], top_v[:, u, h, 0:8], row(k)))
                    chain.did(dve.match_replace(less[:, k, :], top_v[:, u, h, 0:8], row(k), LOWEST))
                split(0)
                chain.hold(held)
                for k, u, h in halves:
                    chain.did(dve.max(top_v[:, u, h, 8:16], less[:, k, :]))
                chain.hold(held)
                for k, u, h in halves:
                    chain.did(dve.max_index(top_i[:, u, h, 8:16], top_v[:, u, h, 8:16], less[:, k, :]))
                shape = [P, 2, TOPK, TOPK]
                chain.did(dve.tensor_tensor(cand[:].rearrange("p u (a b) -> p u a b", a=TOPK),
                                            top_v[:, :, 0, :].unsqueeze(3).broadcast_to(shape),
                                            top_v[:, :, 1, :].unsqueeze(2).broadcast_to(shape), ALU.add))
                split(1)
                chain.hold(held)
                unit = lambda u: top_c[:, u, :]
                for u in range(2):
                    chain.did(dve.max(unit(u)[:, 0:8], cand[:, u, :]))
                chain.hold(held)
                for u in range(2):
                    chain.did(dve.max_index(pos[:, u, 0:8], unit(u)[:, 0:8], cand[:, u, :]))
                    chain.did(dve.match_replace(cand_less[:, u, :], unit(u)[:, 0:8], cand[:, u, :], LOWEST))
                chain.hold(held)
                for u in range(2):
                    chain.did(dve.max(unit(u)[:, 8:16], cand_less[:, u, :]))
                split(2)
                chain.hold(held)
                for u in range(2):
                    chain.did(dve.max_index(pos[:, u, 8:16], unit(u)[:, 8:16], cand_less[:, u, :]))
                chain.wait()
                chain.did(dve.tensor_copy(best[:, ds(2 * i, 2), :], top_c[:]))
                chain.did(dve.tensor_single_scalar(rank[:, 0, :, :], pos[:], 4, ALU.logical_shift_right))
                chain.did(dve.tensor_single_scalar(rank[:, 1, :, :], pos[:], TOPK - 1, ALU.bitwise_and))
                chain.wait()
                for h in range(2):
                    chain.did(dve.tensor_tensor(found[:, h], rank[:, h].unsqueeze(3).broadcast_to(shape),
                                                iota_rank[:].unsqueeze(1).unsqueeze(1).broadcast_to(shape),
                                                ALU.is_equal))
                split(3)
                chain.wait()
                for h in range(2):
                    chain.did(dve.tensor_tensor(found[:, h], found[:, h],
                                                top_i[:, :, h, :].unsqueeze(2).broadcast_to(shape), ALU.mult))
                chain.wait()
                for h, to in enumerate((e1, e2)):
                    chain.did(dve.tensor_reduce(to[:, ds(2 * i, 2), :], found[:, h], AX.X, ALU.add))

            dve.wait_ge(scores_ready, HALVES)
            with dve.Fori(0, TOPK_STEPS) as i:
                chain.enter(i, 41)
                retrieve(i, lambda b: u_split(i, b))
                chain.wait()
            chain.leave(TOPK_STEPS)

            first_best = best[:, :, 0:1]
            chain.did(dve.tensor_copy(denom[:], first_best.rearrange("p u o -> p (u o)")))
            chain.wait()
            dve.tensor_tensor(best[:], best[:], denom[:].unsqueeze(2).broadcast_to([P, UNITS, TOPK]),
                              ALU.subtract).then_inc(shifted, 1)
            for b in range(SLOTS):
                u_split(TOPK_STEPS, b)
            dve.wait_ge(exp_ready, 1)
            chain.did(dve.tensor_reduce(denom[:], best[:], AX.X, ALU.add))
            chain.wait()
            chain.did(dve.reciprocal(denom[:], denom[:]))
            chain.wait()
            dve.tensor_tensor(best[:], best[:], denom[:].unsqueeze(2).broadcast_to([P, UNITS, TOPK]),
                              ALU.mult).then_inc(gates_ready, 1)
            for b in range(SLOTS):
                u_split(TOPK_STEPS + 1, b)

            dve.wait_ge(turned_copied, 3)
            with dve.Fori(0, ONEHOT_STEPS) as s:
                for b in range(SLOTS):
                    for q in range(4 * b, 4 * b + 4):
                        dve.wait_ge(onehots_used, GROUPS_PER_STEP * s + (q + 1))
                        for t in range(TOKENS_PER_GROUP):
                            token = ds(TOKENS_PER_STEP * s + (TOKENS_PER_GROUP * q + t))
                            dve.tensor_scalar(oh1[:, q % SLOTS, t, :], iota_key[:], e1_t[:, token], None,
                                              ALU.is_equal)
                            last = dve.tensor_scalar(oh2[:, q % SLOTS, t, :], iota_key[:], e2_t[:, token],
                                                     gate_t[:, token], ALU.is_equal, ALU.mult)
                        last.then_inc(onehots_ready, 1)
                    u_split(s + ONEHOT_AT, b)
            with dve.Fori(PLAIN_AT, U_STEPS - 1) as step:
                for b in range(SLOTS):
                    u_split(step, b)

            def mask(m, g, b):
                dve.wait_ge(act_loaded[b], 16 * g + 16)
                if b == 0:
                    dve.wait_ge(g_loaded, 16 * g + 16)
                if b < 2:
                    if not isinstance(g, int):
                        dve.wait_ge(al_ready, m - 1)
                else:
                    dve.wait_ge(al_ready, m - 1)
                dve.tensor_tensor(a_f[:, b % 2, :].rearrange("p (c t) -> p c t", t=PIECE),
                                  act_in[:, b, :].rearrange("p (c t) -> p c t", t=PIECE),
                                  g_in[:, :, b, :], ALU.mult).then_inc(af_ready, 1)

            def mask_lo(m, b):
                dve.wait_ge(ah_ready, m + 1)
                dve.tensor_tensor(a_lo[:, b, :], a_f[:, b % 2, :], a_hi[:, b, :].bitcast(F32), ALU.subtract
                                  ).then_inc(al_ready, 1)

            for b in range(SLOTS):
                mask(b, 0, b)
                u_split(U_STEPS - 1, b)
                mask_lo(b, b)
            with dve.Fori(1, KEYS // SLOTS) as g:
                for b in range(SLOTS):
                    mask(SLOTS * g + b, g, b)
                    split_weight(SLOTS * g + (AT_V + b), b)
                    mask_lo(SLOTS * g + b, b)

            for j in range(NB):
                dve.wait_ge(acc_done, j + 1)
                dve.tensor_tensor(h_t[:, j, :], bank[j][:], h_t[:, j, :], ALU.add).then_inc(h2_ready, 1)
            dve.wait_ge(summed, 2 * NB + 1)
            inverse_rms(bank[0][:])
            for j in range(NB):
                dve.scalar_tensor_tensor(out_sb[:, j, :], h_t[:, j, :],
                                         params[:, COL_G_FIN + j:COL_G_FIN + j + 1], row_stat[:],
                                         ALU.mult, ALU.mult).then_inc(out_ready, 1)


def tiles(w):
    return w.reshape(NB, P, -1, P).transpose(2, 1, 0, 3).reshape(-1, P, D)


def per_channel(v):
    return v.reshape(NB, P).T


def kernel(x, norm_mix_g, w_in, conv_w, w_conv_out, pool_w, pool_scale, w_pool_out, w_out, norm_ffn_g,
           w_query, sub_keys, expert_u, expert_v, norm_final_g):
    import concourse.bacc as bacc
    from concourse.bass_utils import run_bass_kernel_spmd

    a = {k: np.asarray(v) for k, v in locals().items() if k not in ("bacc", "run_bass_kernel_spmd")}
    w = tiles(a["w_in"][0]).reshape(6, NB, P, D)
    by_block = lambda *parts: np.stack(parts, 1).reshape(-1, P, D)
    inv_count = np.broadcast_to(1.0 / np.arange(1, PAD + 1, dtype=np.float32), (P, PAD)).astype(np.float32)
    conv_cols = a["conv_w"][0].reshape(TAPS, NB, P).transpose(2, 1, 0).reshape(P, NB * TAPS)
    pool_tiles = a["pool_w"][0].reshape(N_POOL, 2, P, 2 * P).transpose(0, 2, 1, 3).reshape(N_POOL, P, 4 * P)
    arrays = {
        "x_t": a["x"][0].T.reshape(NB, P, T).transpose(1, 0, 2),
        "params": np.concatenate([per_channel(a["norm_mix_g"][0]), per_channel(a["norm_ffn_g"][0]),
                                  per_channel(a["norm_final_g"]), per_channel(a["pool_scale"][0]),
                                  conv_cols, inv_count], 1),
        "w_in": by_block(w[1], w[2], w[0], w[3]),
        "pool": np.concatenate([pool_tiles, np.zeros_like(pool_tiles)], 2),
        "gate": by_block(w[4], w[5], tiles(a["w_conv_out"][0]), tiles(a["w_pool_out"][0])),
        "w_out": tiles(a["w_out"][0]),
        "query": tiles(a["w_query"][0]),
        "keys": a["sub_keys"][0].transpose(3, 0, 1, 2).reshape(P, HALVES, KEYS),
        "u": a["expert_u"][0].reshape(KEYS, KEYS, NB, P).transpose(1, 3, 2, 0).reshape(KEYS, P, D),
        "v": a["expert_v"][0].reshape(KEYS, KEYS, D).transpose(1, 0, 2),
    }
    arrays = {k: np.ascontiguousarray(v) for k, v in arrays.items()}
    nc = bacc.Bacc("TRN2", target_bir_lowering=False, num_devices=1)
    aps = [nc.dram_tensor(k, v.shape, F32, kind="ExternalInput").ap() for k, v in arrays.items()]
    out = nc.dram_tensor("out", (P, NB, T), F32, kind="ExternalOutput").ap()
    act_dram = nc.dram_tensor("act_dram", (KEYS, P, T), F32, kind="Internal").ap()
    g_dram = nc.dram_tensor("g_dram", (P, N_PIECES, KEYS, PIECE), F32, kind="Internal").ap()
    build(nc, *aps, out, act_dram, g_dram)
    got = run_bass_kernel_spmd(nc, [arrays], core_ids=[0]).results[0]["out"]
    return np.ascontiguousarray(got.transpose(1, 0, 2).reshape(D, T).T).reshape(1, T, D)
```

```python
from contextlib import ExitStack

import numpy as np

import concourse.bass as bass
import concourse.mybir as mybir

F32, F32R, U32 = mybir.dt.float32, mybir.dt.float32r, mybir.dt.uint32
ALU, ACT, AX = mybir.AluOpType, mybir.ActivationFunctionType, mybir.AxisListType

P = 128
T = 512
D = 1024
NB = D // P
TAPS = 3
WINDOWS = (2, 4, 8, 16)
PAD = max(WINDOWS)
HEADS = 8
TOPK = 16
KEYS = 128
HALVES = 2 * HEADS
CHUNKS = T // P
UNITS = CHUNKS * HEADS
EPS = 1e-6
SLOTS = 4
LOWEST = -3.4028234663852886e38

N_IN, N_POOL = 4 * NB, len(WINDOWS)
AT_POOL = N_IN
AT_GATE = AT_POOL + N_POOL
AT_OUT = AT_GATE + 4 * NB
AT_QUERY = AT_OUT + NB
AT_U = AT_QUERY + HALVES
AT_V = AT_U + KEYS
N_TILES = AT_V + KEYS

GT = P
DT = T - GT
DENSE = slice(GT, T)
PAIRS = HEADS * TOPK
ROW_SLOTS = 4
TOP_A, LOW_B = 4, 4
WIDE = TOP_A * TOPK
CANDS = WIDE + (TOPK - TOP_A) * LOW_B

TOPK_STEPS = UNITS // 2 - 3
ONEHOT_AT = TOPK_STEPS + 2
ROUND = 2
TOKENS_PER_ROUND = 64
ROUNDS = DT // TOKENS_PER_ROUND
PLAIN_AT = ONEHOT_AT + ROUND * ROUNDS
U_STEPS = KEYS // SLOTS
TOKENS_PER_GROUP = 4
GROUPS_PER_ROUND = TOKENS_PER_ROUND // TOKENS_PER_GROUP
ACT_GROUPS = GROUPS_PER_ROUND * 3 // 4
ROWS_ONEHOT = 2 * 8
ROWS_OF_ROUND = (1, 2) * SLOTS
ROWS_PLAIN = ROWS_ONEHOT + ROUNDS * sum(ROWS_OF_ROUND)
KEPT_STEPS = 3
PIECE = 32
N_PIECES = DT // PIECE

USES_GATE = NB
USES_OUT = USES_GATE + NB
USES_QUERY = USES_OUT + NB // SLOTS
USES_U = USES_QUERY + HALVES // SLOTS
USES_V = USES_U + U_STEPS

COL_G_MIX, COL_G_FFN, COL_G_FIN, COL_SCALE, COL_CONV = 0, 8, 16, 24, 32
COL_INV = COL_CONV + TAPS * NB
N_PARAMS = COL_INV + PAD


def ds(i, n=1):
    return bass.ds(i, n)


class MemoryMap:

    def __init__(self, nc, at):
        self.nc, self.at = nc, at

    def __call__(self, name, shape, dtype=F32):
        size = 4 * int(np.prod(shape[1:]))
        tensor = self.nc.alloc_sbuf_tensor_at(name, shape, dtype, offset=self.at)
        self.at += (size + 31) // 32 * 32
        return tensor


class Chain:

    def __init__(self, engine, sem):
        self.engine, self.sem, self.count, self.base = engine, sem, 0, 0

    def enter(self, i, per_pass):
        self.start, self.per_pass, self.count = self.base + self.count, per_pass, 0
        self.base = i * per_pass + self.start

    def leave(self, passes):
        assert self.count == self.per_pass, (self.count, self.per_pass)
        self.base, self.count = self.start + passes * self.per_pass, 0

    def did(self, instruction):
        instruction.then_inc(self.sem, 1)
        self.count += 1

    def wait(self):
        self.engine.wait_ge(self.sem, self.base + self.count)

    def hold(self, carrier):
        self.wait()
        self.engine.sem_inc(carrier, 1)


def build(nc, x_t, params_d, w_in_d, pool_d, gate_d, w_out_d, query_d, keys_d, u_d, v_d, u_rows, out_d,
          act_dram, g_dram):
    ctx = ExitStack()
    with ctx:
        fixed = MemoryMap(nc, (nc.sbuf_base + 31) // 32 * 32)
        h_t = fixed("h_t", [P, NB, T])
        w_raw = fixed("w_raw", [P, SLOTS, D])
        w_hi = fixed("w_hi", [P, SLOTS, D], F32R)
        w_lo = fixed("w_lo", [P, SLOTS, D], F32R)
        xn_at = fixed.at
        xn_hi = fixed("xn_hi", [P, NB, T], F32R)
        xn_lo = fixed("xn_lo", [P, NB, T], F32R)
        scratch = fixed("scratch", [P, 2, T])
        row_stat = fixed("row_stat", [P, T])
        ones = fixed("ones", [P, P])
        ident = fixed("ident", [P, P])
        ident_r = fixed("ident_r", [P, P], F32R)
        iota_key = fixed("iota_key", [P, KEYS])
        iota_rank = fixed("iota_rank", [P, TOPK], U32)
        params = fixed("params", [P, N_PARAMS])

        front = MemoryMap(nc, fixed.at)
        u_hi = front("u_hi", [P, NB, T], F32R)
        u_lo = front("u_lo", [P, NB, T], F32R)
        mix_hi = front("mix_hi", [P, NB, T], F32R)
        mix_lo = front("mix_lo", [P, NB, T], F32R)
        in_loop = MemoryMap(nc, front.at)
        c_sb = in_loop("c_sb", [P, T])
        z_pad = in_loop("z_pad", [P, TAPS - 1 + T])
        conv = in_loop("conv", [P, 2, T])
        u_f = in_loop("u_f", [P, T])
        p_pad = in_loop("p_pad", [P, PAD + T])
        sums = in_loop("sums", [P, 2, PAD + T])
        pool_f = in_loop("pool_f", [P, T])
        edge = in_loop("edge", [P, PAD])
        mixed_f = in_loop("mixed_f", [P, T])
        gate_loop = MemoryMap(nc, front.at)
        merged_hi = gate_loop("merged_hi", [P, NB, T], F32R)
        merged_lo = gate_loop("merged_lo", [P, NB, T], F32R)
        sig_a = gate_loop("sig_a", [P, T])
        sig_b = gate_loop("sig_b", [P, T])

        peer = MemoryMap(nc, fixed.at)
        keys_t = peer("keys_t", [P, HALVES, KEYS])
        q_sb = peer("q_sb", [P, SLOTS, T])
        scores = peer("scores", [P, CHUNKS, HALVES, KEYS])
        rest = MemoryMap(nc, peer.at)
        act_out = rest("act_out", [P, SLOTS, DT])
        e1_t = rest("e1_t", [P, DT])
        e2_t = rest("e2_t", [P, DT])
        gate_t = rest("gate_t", [P, DT])
        best = rest("best", [P, CHUNKS, HEADS, TOPK])
        e1 = rest("e1", [P, CHUNKS, HEADS, TOPK])
        e2 = rest("e2", [P, CHUNKS, HEADS, TOPK])
        denom = rest("denom", [P, CHUNKS, HEADS])
        expert = rest("expert", [P, 2 * PAIRS + ROW_SLOTS], U32)
        row_index = rest("row_index", [P, ROW_SLOTS], U32)
        rows = rest("rows", [P, ROW_SLOTS, D])
        x_tok = rest("x_tok", [P, D])
        after_topk = MemoryMap(nc, rest.at)
        out_tok = after_topk("out_tok", [P, D])
        dots = after_topk("dots", [P, PAIRS])
        kept = after_topk("kept", [P, KEPT_STEPS - 1, SLOTS, DT])
        top_v = rest("top_v", [P, 2, 2, TOPK])
        top_i = rest("top_i", [P, 2, 2, TOPK], U32)
        less = rest("less", [P, 4, KEYS])
        cand = rest("cand", [P, 2, CANDS])
        cand_less = rest("cand_less", [P, 2, CANDS])
        keyed = rest("keyed", [P, 4, KEYS])
        top_c = rest("top_c", [P, 2, TOPK])
        pos = rest("pos", [P, 2, TOPK], U32)
        rank = rest("rank", [P, 2, 2, TOPK], U32)
        place = rest("place", [P, 4, 2, TOPK], U32)
        found = rest("found", [P, 2, 2, TOPK, TOPK])
        assert max(rest.at, after_topk.at) <= nc.sbuf_usable_end and gate_loop.at <= nc.sbuf_usable_end
        g_build = MemoryMap(nc, fixed.at)
        oh1 = g_build("oh1", [P, SLOTS, TOKENS_PER_GROUP, KEYS])
        oh2 = g_build("oh2", [P, SLOTS, TOKENS_PER_GROUP, KEYS])
        g_sb = g_build("g_sb", [P, 2, KEYS, PIECE])
        assert g_build.at <= peer.at
        v_part = MemoryMap(nc, fixed.at)
        act_in = v_part("act_in", [P, SLOTS, DT])
        g_in = [region(f"g_in{k}", [P, N_PIECES, SLOTS, PIECE])
                for k, region in enumerate((v_part, MemoryMap(nc, xn_at)))]
        a_f = v_part("a_f", [P, 2, DT])
        a_hi = v_part("a_hi", [P, SLOTS, DT], F32R)
        a_lo = v_part("a_lo", [P, SLOTS, DT], F32R)
        assert v_part.at <= peer.at
        out_sb = MemoryMap(nc, fixed.at)("out_sb", [P, NB, T])

        bank = [ctx.enter_context(nc.psum_tensor(f"bank{b}", [P, T], F32)) for b in range(8)]

        def sem(name):
            return ctx.enter_context(nc.semaphore(name))

        x_loaded = [sem(f"x_loaded{k}") for k in range(2)]
        params_loaded = sem("params_loaded")
        keys_loaded = sem("keys_loaded")
        raw_loaded = [sem(f"raw_loaded{k}") for k in range(SLOTS)]
        hi_done = sem("hi_done")
        lo_done = sem("lo_done")
        job_done = sem("job_done")
        bank_free = [sem(f"bank_free{b}") for b in range(SLOTS)]
        consts = sem("consts")
        squared = sem("squared")
        summed = sem("summed")
        h_ready = sem("h_ready")
        xn_f = sem("xn_f")
        xn_h = sem("xn_h")
        xn_l = sem("xn_l")
        c_copied, p_copied = sem("c_copied"), sem("p_copied")
        uf_ready, uh_ready, ul_ready = sem("uf_ready"), sem("uh_ready"), sem("ul_ready")
        pf_ready, ph_ready, pl_ready = sem("pf_ready"), sem("ph_ready"), sem("pl_ready")
        mf_ready, mh_ready, ml_ready = sem("mf_ready"), sem("mh_ready"), sem("ml_ready")
        sigmoids = sem("sigmoids")
        gf_ready, gh_ready, gl_ready = sem("gf_ready"), sem("gh_ready"), sem("gl_ready")
        q_ready, scored, scores_ready = sem("q_ready"), sem("scored"), sem("scores_ready")
        act_ready = sem("act_ready")
        act_stored = [sem(f"act_stored{b}") for b in range(SLOTS)]
        shifted, exp_ready, gates_ready = sem("shifted"), sem("exp_ready"), sem("gates_ready")
        turned, turned_copied = sem("turned"), sem("turned_copied")
        gaps_ready = sem("gaps_ready")
        oh1_ready = sem("oh1_ready")
        oh2_ready = sem("oh2_ready")
        onehots_used = sem("onehots_used")
        g_copied = sem("g_copied")
        g_stored = [sem(f"g_stored{k}") for k in range(2)]
        act_loaded = [sem(f"act_loaded{b}") for b in range(SLOTS)]
        g_loaded = sem("g_loaded")
        af_ready, ah_ready, al_ready = sem("af_ready"), sem("ah_ready"), sem("al_ready")
        acc_done = sem("acc_done")
        h2_ready, out_ready, out_stored = sem("h2_ready"), sem("out_ready"), sem("out_stored")
        ident_ready = sem("ident_ready")
        x_turned, x_tok_ready = sem("x_turned"), sem("x_tok_ready")
        rows_loaded = [sem(f"rows_loaded{k}") for k in range(ROW_SLOTS)]
        wait_carried = sem("wait_carried")
        rows_used = sem("rows_used")
        dots_gelu = sem("dots_gelu")
        tok_done = sem("tok_done")
        var_ready, root_ready = sem("var_ready"), sem("root_ready")
        held = sem("held")
        dve_step = sem("dve_step")

        block = ctx.enter_context(nc.Block())

        @block.sync
        def _(sp):
            def load_raw(source, k, n, slot):
                if not isinstance(n, int) or n >= SLOTS:
                    sp.wait_ge(lo_done, n - SLOTS + 1)
                sp.dma_start(w_raw[:, slot, :], source[ds(k), :, :].rearrange("o p d -> (o p) d")
                             ).then_inc(raw_loaded[slot], 16)

            def load_all(source, first, count, start=0):
                with sp.Fori(start // SLOTS, count // SLOTS) as i:
                    for b in range(SLOTS):
                        load_raw(source, SLOTS * i + b, SLOTS * i + (first + b), b)

            for half in range(2):
                sp.dma_start(h_t[:, 4 * half:4 * half + 4, :], x_t[:, 4 * half:4 * half + 4, :]
                             ).then_inc(x_loaded[half], 16)
            sp.dma_start(params[:], params_d).then_inc(params_loaded, 16)
            for b in range(SLOTS):
                load_raw(w_in_d, b, b, b)
            load_all(w_in_d, 0, N_IN, start=SLOTS)
            load_all(pool_d, AT_POOL, N_POOL)
            load_all(gate_d, AT_GATE, 4 * NB)
            load_all(w_out_d, AT_OUT, NB)
            for k in range(HALVES):
                if k == 2 * SLOTS:
                    sp.wait_ge(job_done, AT_QUERY)
                    sp.dma_start(keys_t[:], keys_d).then_inc(keys_loaded, 16)
                load_raw(query_d, k, AT_QUERY + k, k % SLOTS)
            load_all(u_d, AT_U, KEYS)

            for k in range(2):
                sp.wait_ge(g_stored[k], 16 * N_PIECES // 2)

            def load_v_group(g, parity):
                if isinstance(g, int):
                    e2 = SLOTS * (g - KEPT_STEPS) % KEYS
                else:
                    e2 = SLOTS * (g - KEPT_STEPS)
                for b in range(SLOTS):
                    load_raw(v_d, e2 + b, SLOTS * g + (AT_V + b), b)
                    if not isinstance(g, int) or g >= KEPT_STEPS:
                        if not isinstance(g, int) or g > KEPT_STEPS:
                            sp.wait_ge(af_ready, SLOTS * g + (b - SLOTS + 1))
                        sp.wait_ge(act_stored[b], 16 * g + (16 - 16 * KEPT_STEPS))
                        sp.dma_start(act_in[:, b, :],
                                     act_dram[ds(e2 + b), :, :].rearrange("o p t -> (o p) t")
                                     ).then_inc(act_loaded[b], 16)
                    if b == 0:
                        if not isinstance(g, int) or g >= 2:
                            sp.wait_ge(af_ready, SLOTS * g - SLOTS)
                        elif g == 1:
                            sp.wait_ge(job_done, AT_V)
                        sp.dma_start(g_in[parity][:], g_dram[:, :, ds(e2, SLOTS), :]).then_inc(g_loaded, 16)

            for g in range(4):
                load_v_group(g, g % 2)
            with sp.Fori(2, U_STEPS // 2) as i:
                for k in range(2):
                    load_v_group(2 * i + k, k)

            for j in range(NB):
                sp.wait_ge(out_ready, j + 1)
                sp.dma_start(out_d[:, j, :], out_sb[:, j, :]).then_inc(out_stored, 16)
            sp.wait_ge(out_stored, 16 * NB)

        @block.gpsimd
        def _(pool):
            pool.memset(ones[:], 1.0).then_inc(consts, 1)
            pool.memset(z_pad[:, 0:TAPS - 1], 0.0).then_inc(consts, 1)
            pool.memset(p_pad[:, 0:PAD], 0.0).then_inc(consts, 1)
            pool.memset(ident[:], 0.0).then_inc(consts, 1)
            pool.iota(iota_rank[:], pattern=[[1, TOPK]], base=0, channel_multiplier=0).then_inc(consts, 1)
            pool.iota(iota_key[:], pattern=[[1, KEYS]], base=0, channel_multiplier=0,
                      allow_small_or_imprecise_dtypes=True).then_inc(consts, 1)
            pool.wait_ge(consts, 6)
            pool.affine_select(out=ident[:], in_=ident[:], compare_op=ALU.not_equal, fill=1.0, base=0,
                               pattern=[[-1, P]], channel_multiplier=1).then_inc(consts, 1)

            def gather(table, r, slot):
                pool.wait_ge(rows_used, r + 1)
                pool.sem_inc(wait_carried, 1)
                pool.indirect_dma_start(out=rows[:, slot, :], out_offset=None,
                                        in_=table.rearrange("a p d -> (a p) d"),
                                        in_offset=bass.IndirectOffsetOnAxis(ap=row_index[:, slot:slot + 1], axis=0)
                                        ).then_inc(rows_loaded[slot], 16)

            for table, at in ((u_rows, 0), (v_d, PAIRS)):
                with pool.Fori(0, PAIRS // ROW_SLOTS) as g:
                    for slot in range(ROW_SLOTS):
                        gather(table, ROW_SLOTS * g + (at + slot), slot)

        @block.scalar
        def _(act):
            def root(count):
                act.wait_ge(var_ready, count)
                act.activation(scratch[:, 0, :], row_stat[:], ACT.Sqrt).then_inc(root_ready, 1)

            def split_weight(n, slot, times):
                act.wait_ge(raw_loaded[slot], 16 * times)
                if not isinstance(n, int) or n >= SLOTS:
                    act.wait_ge(job_done, n - SLOTS + 1)
                act.activation(w_hi[:, slot, :], w_raw[:, slot, :], ACT.Copy).then_inc(hi_done, 1)

            def norm_hi(base):
                for j in range(NB):
                    act.wait_ge(xn_f, base + j + 1)
                    act.activation(xn_hi[:, j, :], scratch[:, j % 2, :], ACT.Copy).then_inc(xn_h, 1)

            for j in range(NB):
                if j % 4 == 0:
                    act.wait_ge(x_loaded[j // 4], 16)
                if j >= 2:
                    act.wait_ge(summed, j - 1)
                act.activation(scratch[:, j % 2, :], h_t[:, j, :], ACT.Square).then_inc(squared, 1)
            split_weight(0, 0, 1)
            root(1)
            split_weight(1, 1, 1)
            norm_hi(0)
            split_weight(2, 2, 1)
            split_weight(3, 3, 1)

            with act.Fori(0, NB) as i:
                act.wait_ge(job_done, SLOTS * i + 1)
                act.activation(p_pad[:, PAD:], bank[0][:], ACT.Copy).then_inc(p_copied, 1)
                split_weight(SLOTS * i + 4, 0, i + 2)
                act.wait_ge(job_done, SLOTS * i + 2)
                act.activation(c_sb[:], bank[1][:], ACT.Copy).then_inc(c_copied, 1)
                split_weight(SLOTS * i + 5, 1, i + 2)
                act.wait_ge(pf_ready, i + 1)
                act.activation(mix_hi[:, ds(i), :], pool_f[:], ACT.Copy).then_inc(ph_ready, 1)
                split_weight(SLOTS * i + 6, 2, i + 2)
                split_weight(SLOTS * i + 7, 3, i + 2)
                act.wait_ge(uf_ready, i + 1)
                act.activation(u_hi[:, ds(i), :], u_f[:], ACT.Copy).then_inc(uh_ready, 1)

            for g in range(N_POOL):
                act.wait_ge(job_done, AT_POOL + g + 1)
                for jo in range(2):
                    j = 2 * g + jo
                    if j >= 1:
                        act.wait_ge(ml_ready, j)
                    act.activation(mixed_f[:], bank[4 + 2 * (g % 2) + jo][:], ACT.Copy,
                                   scale=params[:, COL_SCALE + j:COL_SCALE + j + 1]).then_inc(mf_ready, 1)
                    act.wait_ge(mf_ready, j + 1)
                    act.activation(mix_hi[:, j, :], mixed_f[:], ACT.Copy).then_inc(mh_ready, 1)
                split_weight(AT_GATE + g, g, NB + 2)

            with act.Fori(0, NB) as i:
                for b, sig in ((0, sig_a), (1, sig_b)):
                    act.wait_ge(job_done, SLOTS * i + (AT_GATE + b + 1))
                    act.activation(sig[:], bank[b][:], ACT.Sigmoid).then_inc(sigmoids, 1)
                    split_weight(SLOTS * i + (AT_GATE + SLOTS + b), b, i + (NB + 3))
                for b in (2, 3):
                    split_weight(SLOTS * i + (AT_GATE + SLOTS + b), b, i + (NB + 3))
                act.wait_ge(gf_ready, i + 1)
                act.activation(merged_hi[:, ds(i), :], scratch[:, 0, :], ACT.Copy).then_inc(gh_ready, 1)

            with act.Fori(0, NB // SLOTS) as i:
                for b in range(SLOTS):
                    split_weight(SLOTS * i + (AT_OUT + SLOTS + b), b, i + (2 * NB + 3))
                    act.wait_ge(h_ready, SLOTS * i + (b + 1))
                    act.activation(scratch[:, b % 2, :], h_t[:, ds(SLOTS * i + b), :], ACT.Square).then_inc(squared, 1)
            root(2)
            norm_hi(NB)

            with act.Fori(0, HALVES // SLOTS) as i:
                def copy_scores(b):
                    act.wait_ge(scored, SLOTS * i + (b + 1))
                    act.activation(scores[:, :, ds(SLOTS * i + b), :].rearrange("p c o n -> p c (o n)"),
                                   bank[4 + b][:].rearrange("p (c n) -> p c n", c=CHUNKS),
                                   ACT.Copy).then_inc(scores_ready, 1)

                for b in range(SLOTS):
                    act.wait_ge(job_done, SLOTS * i + (AT_QUERY + b + 1))
                    act.activation(q_sb[:, b, :], bank[b][:], ACT.Copy).then_inc(q_ready, 1)
                    split_weight(SLOTS * i + (AT_QUERY + SLOTS + b), b, i + (AT_QUERY // SLOTS + 2))
                    if b >= 1:
                        copy_scores(b - 1)
                copy_scores(SLOTS - 1)

            for k in range(2):
                act.wait_ge(x_turned, k + 1)
                act.activation(x_tok[:, k * T:(k + 1) * T], bank[4 + k][:], ACT.Copy).then_inc(x_tok_ready, 1)

            def gelu_tile(step, b):
                act.wait_ge(job_done, SLOTS * step + (AT_U + b + 1))
                stored = not isinstance(step, int) or step < U_STEPS - KEPT_STEPS
                to = act_out[:, b, :]
                if not isinstance(step, int) or 0 < step < U_STEPS - KEPT_STEPS:
                    act.wait_ge(act_stored[b], 16 * step)
                elif step == U_STEPS - 1:
                    act.wait_ge(act_stored[b], 16 * (U_STEPS - KEPT_STEPS))
                elif not stored:
                    to = kept[:, step - (U_STEPS - KEPT_STEPS), b, :]
                act.activation(to, bank[b][:, DENSE], ACT.Gelu).then_inc(act_ready, 1)
                split_weight(SLOTS * step + (AT_U + SLOTS + b), b, step + (AT_U // SLOTS + 2))
                if stored:
                    act.wait_ge(act_ready, SLOTS * step + (b + 1))
                    act.dma_start(act_dram[ds(SLOTS * step + b), :, :].rearrange("o p t -> (o p) t"),
                                  act_out[:, b, :]).then_inc(act_stored[b], 16)

            key_gap = lambda q: scratch[:, q % 2, :].rearrange("p (t n) -> p t n", n=KEYS)

            def one_hots(s, q):
                if q >= GROUPS_PER_ROUND:
                    s, q = s + 1, q - GROUPS_PER_ROUND
                if q % 4 == 3:
                    return
                n = ACT_GROUPS * s + (q - q // 4)
                gap = key_gap(q - q // 4)
                act.wait_ge(onehots_used, GROUPS_PER_ROUND * s + (q + 1))
                if not isinstance(n, int) or n >= 2:
                    act.wait_ge(oh1_ready, n - 1)
                for t in range(TOKENS_PER_GROUP):
                    last = act.activation(gap[:, t, :], iota_key[:], ACT.Abs, scale=-1.0,
                                          bias=e1_t[:, ds(TOKENS_PER_ROUND * s + (TOKENS_PER_GROUP * q + t))])
                last.then_inc(gaps_ready, 1)
                act.wait_ge(gaps_ready, n + 1)
                act.activation(oh1[:, q % SLOTS, :, :], gap, ACT.Relu, scale=-1.0,
                               bias=ones[:, 0:1]).then_inc(oh1_ready, 1)

            def copy_g(s, q):
                k, t = q // 8, TOKENS_PER_GROUP * (q % 8)
                if q % 8 == 0 and (not isinstance(s, int) or s > 0):
                    act.wait_ge(g_stored[k], 16 * s)
                act.wait_ge(onehots_used, GROUPS_PER_ROUND * s + (SLOTS + q + 1))
                act.activation(g_sb[:, k, :, t:t + TOKENS_PER_GROUP].rearrange("p e t -> p t e"),
                               bank[4 + q % SLOTS][:].rearrange("p (t e) -> p t e", e=KEYS),
                               ACT.Copy).then_inc(g_copied, 1)

            def store_g(s, k):
                act.wait_ge(g_copied, GROUPS_PER_ROUND * s + (SLOTS + 8 * (k + 1)))
                act.dma_start(g_dram[:, ds(2 * s + k), :, :].rearrange("p o e t -> p (o e) t"),
                              g_sb[:, k, :, :]).then_inc(g_stored[k], 16)

            def g_round(s, last=False):
                for b in range(ROUND * SLOTS):
                    gelu_tile(ROUND * s + (ONEHOT_AT + b // SLOTS), b % SLOTS)
                    for q in (2 * b, 2 * b + 1):
                        if not last or q + 2 < GROUPS_PER_ROUND:
                            one_hots(s, q + 2)
                        copy_g(s, q)
                    if b % SLOTS == SLOTS - 1:
                        store_g(s, b // SLOTS)

            for b in range(SLOTS):
                gelu_tile(0, b)
            with act.Fori(1, TOPK_STEPS) as step:
                for b in range(SLOTS):
                    gelu_tile(step, b)
            for b in range(SLOTS // 2):
                gelu_tile(TOPK_STEPS, b)
            act.wait_ge(shifted, 1)
            act.activation(best[:], best[:], ACT.Exp).then_inc(exp_ready, 1)
            for b in range(SLOTS // 2, SLOTS):
                gelu_tile(TOPK_STEPS, b)
            for b in range(SLOTS // 2):
                gelu_tile(TOPK_STEPS + 1, b)
            for k, turned_to in enumerate((e1_t, e2_t, gate_t)):
                act.wait_ge(turned, k + 1)
                act.activation(turned_to[:], bank[4 + k][:, 0:DT], ACT.Copy).then_inc(turned_copied, 1)
            act.sem_inc(g_copied, SLOTS)
            act.wait_ge(turned_copied, 1)
            for b in range(SLOTS // 2, SLOTS):
                gelu_tile(TOPK_STEPS + 1, b)
                one_hots(0, b - SLOTS // 2)
            g_round(0)
            with act.Fori(1, ROUNDS - 1) as s:
                g_round(s)
            g_round(ROUNDS - 1, last=True)
            with act.Fori(PLAIN_AT, U_STEPS - KEPT_STEPS) as step:
                for b in range(SLOTS):
                    gelu_tile(step, b)
            for step in range(U_STEPS - KEPT_STEPS, U_STEPS - 1):
                for b in range(SLOTS):
                    gelu_tile(step, b)

            def split_a(m, b):
                act.wait_ge(af_ready, m + 1)
                act.activation(a_hi[:, b, :], a_f[:, b % 2, :], ACT.Copy).then_inc(ah_ready, 1)

            for b in range(SLOTS):
                gelu_tile(U_STEPS - 1, b)
                split_a(b, b)
            act.wait_ge(rows_used, ROW_SLOTS + PAIRS)
            act.activation(dots[:], dots[:], ACT.Gelu).then_inc(dots_gelu, 1)
            with act.Fori(1, U_STEPS) as g:
                for b in range(SLOTS):
                    split_weight(SLOTS * g + (AT_V + b), b, g + (AT_V // SLOTS + 1))
                    split_a(SLOTS * g + b, b)

            for j in range(NB):
                act.wait_ge(h2_ready, j + 1)
                if j >= 2:
                    act.wait_ge(summed, NB + 1 + j - 1)
                act.activation(scratch[:, j % 2, :], h_t[:, j, :], ACT.Square).then_inc(squared, 1)
            root(3)

        @block.tensor
        def _(pe):
            def k_block(tensor, slot, k):
                return tensor[:, slot, k * P:(k + 1) * P]

            def tile_product(n, b, uses, act_hi, act_lo, parts=None, base=0, tokens=slice(0, T)):
                pe.wait_ge(lo_done, n + 1)
                pe.wait_ge(bank_free[b], uses)
                for k in range(NB):
                    if parts is not None:
                        pe.wait_ge(parts, base + k + 1)
                    hi, lo = k_block(w_hi, b, k), k_block(w_lo, b, k)
                    out = bank[b][:, tokens]
                    pe.matmul(out, hi, act_hi[:, k, tokens], start=k == 0, stop=False)
                    pe.matmul(out, hi, act_lo[:, k, tokens], start=False, stop=False)
                    last = pe.matmul(out, lo, act_hi[:, k, tokens], start=False, stop=k == NB - 1)
                last.then_inc(job_done, 1)

            pe.wait_ge(consts, 7)
            for j in range(NB):
                pe.wait_ge(squared, j + 1)
                pe.matmul(bank[4][:], ones[:], scratch[:, j % 2, :], start=j == 0, stop=j == NB - 1
                          ).then_inc(summed, 1)

            with pe.Fori(0, NB) as i:
                for b in range(SLOTS):
                    tile_product(SLOTS * i + b, b, i + 1, xn_hi, xn_lo, xn_l if b == 0 else None)

            pe.wait_ge(pl_ready, NB)
            for g in range(N_POOL):
                pe.wait_ge(lo_done, AT_POOL + g + 1)
                if g >= 2:
                    pe.wait_ge(mf_ready, 2 * (g - 1))
                for jo in range(2):
                    to = bank[4 + 2 * (g % 2) + jo]
                    for ki in range(2):
                        hi, lo = k_block(w_hi, g, 2 * ki + jo), k_block(w_lo, g, 2 * ki + jo)
                        x_hi, x_lo = mix_hi[:, 2 * g + ki, :], mix_lo[:, 2 * g + ki, :]
                        pe.matmul(to[:], hi, x_hi, start=ki == 0, stop=False)
                        pe.matmul(to[:], hi, x_lo, start=False, stop=False)
                        last = pe.matmul(to[:], lo, x_hi, start=False, stop=ki == 1)
                last.then_inc(job_done, 1)

            with pe.Fori(0, NB) as i:
                for b, (a_h, a_l) in enumerate(((xn_hi, xn_lo), (xn_hi, xn_lo), (u_hi, u_lo), (mix_hi, mix_lo))):
                    if b == 2:
                        pe.wait_ge(ul_ready, NB)
                        pe.wait_ge(ml_ready, NB)
                    tile_product(SLOTS * i + (AT_GATE + b), b, i + (USES_GATE + 1), a_h, a_l)

            with pe.Fori(0, NB // SLOTS) as i:
                for b in range(SLOTS):
                    tile_product(SLOTS * i + (AT_OUT + b), b, i + (USES_OUT + 1), merged_hi, merged_lo,
                                 gl_ready if b == 0 else None)
            pe.wait_ge(h_ready, NB + 1)
            pe.matmul(bank[4][:], ones[:], row_stat[:], start=True, stop=True).then_inc(summed, 1)

            pe.wait_ge(keys_loaded, 16)
            with pe.Fori(0, HALVES // SLOTS) as i:
                def score(b):
                    pe.wait_ge(q_ready, SLOTS * i + (b + 1))
                    for c in range(CHUNKS):
                        last = pe.matmul(bank[4 + b][:, c * KEYS:(c + 1) * KEYS], q_sb[:, b, c * P:(c + 1) * P],
                                         keys_t[:, ds(SLOTS * i + b), :].rearrange("p o n -> p (o n)"),
                                         start=True, stop=True)
                    last.then_inc(scored, 1)

                for b in range(SLOTS):
                    tile_product(SLOTS * i + (AT_QUERY + b), b, i + (USES_QUERY + 1), xn_hi, xn_lo,
                                 xn_l if b == 0 else None, NB)
                    if b >= 1:
                        score(b - 1)
                score(SLOTS - 1)

            pe.wait_ge(scores_ready, HALVES)
            pe.wait_ge(ident_ready, 1)
            for k in range(2):
                for j in range(4 * k, 4 * k + 4):
                    at = bank[4 + k][:, (j - 4 * k) * P:(j - 4 * k + 1) * P]
                    pe.matmul(at, xn_hi[:, j, 0:GT], ident_r[:], start=True, stop=False)
                    last = pe.matmul(at, xn_lo[:, j, 0:GT], ident_r[:], start=False, stop=True)
                last.then_inc(x_turned, 1)

            def u_tile(step, b):
                tile_product(SLOTS * step + (AT_U + b), b, step + (USES_U + 1), xn_hi, xn_lo, tokens=DENSE)

            with pe.Fori(0, ONEHOT_AT - 1) as step:
                for b in range(SLOTS):
                    u_tile(step, b)
            for b in range(SLOTS // 2):
                u_tile(ONEHOT_AT - 1, b)
            pe.wait_ge(x_tok_ready, 2)
            pe.wait_ge(gates_ready, 1)
            for k, tensor in enumerate((e1, e2, best)):
                for c in range(1, CHUNKS):
                    last = pe.transpose(bank[4 + k][:, (c - 1) * P:c * P],
                                        tensor[:, c, :, :].rearrange("p h r -> p (h r)"), ident[:])
                last.then_inc(turned, 1)
            for b in range(SLOTS // 2, SLOTS):
                u_tile(ONEHOT_AT - 1, b)

            pe.sem_inc(onehots_used, SLOTS)
            with pe.Fori(0, ROUNDS) as s:
                for b in range(ROUND * SLOTS):
                    u_tile(ROUND * s + (ONEHOT_AT + b // SLOTS), b % SLOTS)
                    for q in (2 * b, 2 * b + 1):
                        if q % 4 != 3:
                            pe.wait_ge(oh1_ready, ACT_GROUPS * s + (q - q // 4 + 1))
                        pe.wait_ge(oh2_ready, GROUPS_PER_ROUND * s + (q + 1))
                        pe.wait_ge(g_copied, GROUPS_PER_ROUND * s + (q + 1))
                        for t in range(TOKENS_PER_GROUP):
                            last = pe.matmul(bank[4 + q % SLOTS][:, t * KEYS:(t + 1) * KEYS],
                                             oh1[:, q % SLOTS, t, :], oh2[:, q % SLOTS, t, :],
                                             start=True, stop=True)
                        last.then_inc(onehots_used, 1)
            with pe.Fori(PLAIN_AT, U_STEPS) as step:
                for b in range(SLOTS):
                    u_tile(step, b)

            def v_tile(g, b, first=False, final=False):
                pe.wait_ge(lo_done, SLOTS * g + (AT_V + b + 1))
                pe.wait_ge(al_ready, SLOTS * g + (b + 1))
                for j in range(NB):
                    if first and j < SLOTS:
                        pe.wait_ge(bank_free[j], USES_V + 1)
                    hi, lo = k_block(w_hi, b, j), k_block(w_lo, b, j)
                    out = bank[j][:, DENSE]
                    pe.matmul(out, hi, a_hi[:, b, :], start=first, stop=False)
                    pe.matmul(out, hi, a_lo[:, b, :], start=False, stop=False)
                    last = pe.matmul(out, lo, a_hi[:, b, :], start=False, stop=final)
                last.then_inc(job_done, 1)

            pe.wait_ge(g_copied, SLOTS + DT // TOKENS_PER_GROUP)
            for b in range(SLOTS):
                v_tile(0, b, first=b == 0)
            with pe.Fori(1, U_STEPS - 1) as g:
                for b in range(SLOTS):
                    v_tile(g, b)
            for b in range(SLOTS):
                v_tile(U_STEPS - 1, b, final=b == SLOTS - 1)

            pe.wait_ge(tok_done, 1)
            for j in range(NB):
                pe.transpose(bank[j][:, 0:GT], out_tok[:, j * P:(j + 1) * P], ident[:]).then_inc(acc_done, 1)

            for j in range(NB):
                pe.wait_ge(squared, 2 * NB + j + 1)
                pe.matmul(bank[0][:], ones[:], scratch[:, j % 2, :], start=j == 0, stop=j == NB - 1
                          ).then_inc(summed, 1)

        @block.vector
        def _(dve):
            chain = Chain(dve, dve_step)
            norms = [0]

            def split_weight(n, slot):
                dve.wait_ge(hi_done, n + 1)
                dve.tensor_tensor(w_lo[:, slot, :], w_raw[:, slot, :], w_hi[:, slot, :].bitcast(F32),
                                  ALU.subtract).then_inc(lo_done, 1)

            def inverse_rms(source):
                dve.tensor_scalar(row_stat[:], source, 1.0 / D, EPS, ALU.mult, ALU.add).then_inc(var_ready, 1)
                norms[0] += 1
                dve.wait_ge(root_ready, norms[0])
                y, t = scratch[:, 1, :], scratch[:, 0, :]
                chain.did(dve.reciprocal(y, t))
                chain.wait()
                chain.did(dve.tensor_tensor(t, y, y, ALU.mult))
                chain.wait()
                chain.did(dve.tensor_tensor(t, t, row_stat[:], ALU.mult))
                chain.wait()
                chain.did(dve.tensor_scalar(t, t, -0.5, 1.5, ALU.mult, ALU.add))
                chain.wait()
                chain.did(dve.tensor_tensor(row_stat[:], y, t, ALU.mult))
                chain.wait()

            def norm_apply(base, gain_col):
                def lo(j):
                    dve.wait_ge(xn_h, base + j + 1)
                    dve.tensor_tensor(xn_lo[:, j, :], scratch[:, j % 2, :], xn_hi[:, j, :].bitcast(F32),
                                      ALU.subtract).then_inc(xn_l, 1)

                for j in range(NB):
                    if j >= 2:
                        dve.wait_ge(xn_l, base + j - 1)
                    dve.scalar_tensor_tensor(scratch[:, j % 2, :], h_t[:, j, :],
                                             params[:, gain_col + j:gain_col + j + 1], row_stat[:],
                                             ALU.mult, ALU.mult).then_inc(xn_f, 1)
                    if j >= 1:
                        lo(j - 1)
                lo(NB - 1)

            for b in range(SLOTS):
                dve.sem_inc(bank_free[b], 1)
            dve.wait_ge(params_loaded, 16)
            dve.wait_ge(summed, NB)
            inverse_rms(bank[4][:])
            split_weight(0, 0)
            norm_apply(0, COL_G_MIX)
            for b in range(1, SLOTS):
                split_weight(b, b)
            dve.wait_ge(consts, 7)
            dve.tensor_copy(ident_r[:], ident[:]).then_inc(ident_ready, 1)

            def in_block(i, window):
                tap = lambda k: params[:, ds(TAPS * i + (COL_CONV + k))]
                dve.wait_ge(p_copied, i + 1)
                dve.sem_inc(bank_free[0], 1)
                source, width, side = p_pad[:], 1, 0
                while width < window:
                    begin = 2 * width - 1
                    chain.did(dve.tensor_tensor(sums[:, side, begin:], source[:, begin:],
                                                source[:, begin - width:PAD + T - width], ALU.add))
                    chain.wait()
                    source, width, side = sums[:, side, :], 2 * width, 1 - side
                chain.did(dve.tensor_tensor(edge[:, 0:window], source[:, PAD:PAD + window],
                                            params[:, COL_INV:COL_INV + window], ALU.mult))
                chain.did(dve.scalar_tensor_tensor(pool_f[:], source[:, PAD:], 1.0 / window, p_pad[:, PAD:],
                                                   ALU.mult, ALU.subtract))
                chain.wait()
                dve.tensor_tensor(pool_f[:, 0:window], edge[:, 0:window], p_pad[:, PAD:PAD + window],
                                  ALU.subtract).then_inc(pf_ready, 1)
                split_weight(SLOTS * i + 4, 0)
                dve.wait_ge(ph_ready, i + 1)
                dve.tensor_tensor(mix_lo[:, ds(i), :], pool_f[:], mix_hi[:, ds(i), :].bitcast(F32),
                                  ALU.subtract).then_inc(pl_ready, 1)
                split_weight(SLOTS * i + 5, 1)
                dve.wait_ge(c_copied, i + 1)
                dve.sem_inc(bank_free[1], 1)
                dve.wait_ge(job_done, SLOTS * i + 3)
                chain.did(dve.tensor_tensor(z_pad[:, TAPS - 1:], bank[2][:], c_sb[:], ALU.mult))
                split_weight(SLOTS * i + 6, 2)
                chain.wait()
                dve.sem_inc(bank_free[2], 1)
                chain.did(dve.tensor_scalar(conv[:, 0, :], z_pad[:, 0:T], tap(0), None, ALU.mult))
                chain.wait()
                chain.did(dve.scalar_tensor_tensor(conv[:, 1, :], z_pad[:, 1:1 + T], tap(1), conv[:, 0, :],
                                                   ALU.mult, ALU.add))
                chain.wait()
                chain.did(dve.scalar_tensor_tensor(conv[:, 0, :], z_pad[:, 2:2 + T], tap(2), conv[:, 1, :],
                                                   ALU.mult, ALU.add))
                dve.wait_ge(job_done, SLOTS * i + 4)
                chain.wait()
                dve.tensor_tensor(u_f[:], bank[3][:], conv[:, 0, :], ALU.mult).then_inc(uf_ready, 1)
                split_weight(SLOTS * i + 7, 3)
                dve.wait_ge(uh_ready, i + 1)
                dve.sem_inc(bank_free[3], 1)
                dve.tensor_tensor(u_lo[:, ds(i), :], u_f[:], u_hi[:, ds(i), :].bitcast(F32), ALU.subtract
                                  ).then_inc(ul_ready, 1)

            for g, window in enumerate(WINDOWS):
                with dve.Fori(2 * g, 2 * g + 2) as i:
                    chain.enter(i - 2 * g, 4 + (window.bit_length() - 1) + 2)
                    in_block(i, window)
                chain.leave(2)

            for g in range(N_POOL):
                for jo in range(2):
                    j = 2 * g + jo
                    dve.wait_ge(mh_ready, j + 1)
                    dve.tensor_tensor(mix_lo[:, j, :], mixed_f[:], mix_hi[:, j, :].bitcast(F32), ALU.subtract
                                      ).then_inc(ml_ready, 1)
                split_weight(AT_GATE + g, g)

            with dve.Fori(0, NB) as i:
                chain.enter(i, 2)
                for b in range(2):
                    dve.wait_ge(sigmoids, 2 * i + (b + 1))
                    dve.sem_inc(bank_free[b], 1)
                    split_weight(SLOTS * i + (AT_GATE + SLOTS + b), b)
                for b, sig in ((2, sig_a), (3, sig_b)):
                    dve.wait_ge(job_done, SLOTS * i + (AT_GATE + b + 1))
                    chain.did(dve.tensor_tensor(sig[:], bank[b][:], sig[:], ALU.mult))
                    split_weight(SLOTS * i + (AT_GATE + SLOTS + b), b)
                    chain.wait()
                    dve.sem_inc(bank_free[b], 1)
                dve.tensor_tensor(scratch[:, 0, :], sig_a[:], sig_b[:], ALU.add).then_inc(gf_ready, 1)
                dve.wait_ge(gh_ready, i + 1)
                dve.tensor_tensor(merged_lo[:, ds(i), :], scratch[:, 0, :], merged_hi[:, ds(i), :].bitcast(F32),
                                  ALU.subtract).then_inc(gl_ready, 1)
            chain.leave(NB)

            chain.did(dve.memset(row_stat[:], 0.0))
            with dve.Fori(0, NB // SLOTS) as i:
                chain.enter(i, SLOTS)
                for b in range(SLOTS):
                    block_j = h_t[:, ds(SLOTS * i + b), :].rearrange("p o t -> p (o t)")
                    dve.wait_ge(job_done, SLOTS * i + (AT_OUT + b + 1))
                    dve.tensor_tensor(block_j, bank[b][:], block_j, ALU.add).then_inc(h_ready, 1)
                    split_weight(SLOTS * i + (AT_OUT + SLOTS + b), b)
                    dve.wait_ge(squared, SLOTS * i + (NB + b + 1))
                    dve.sem_inc(bank_free[b], 1)
                    chain.wait()
                    chain.did(dve.tensor_tensor(row_stat[:], row_stat[:], scratch[:, b % 2, :], ALU.add))
            chain.leave(NB // SLOTS)
            chain.wait()
            dve.sem_inc(h_ready, 1)
            dve.wait_ge(summed, NB + 1)
            inverse_rms(bank[4][:])
            norm_apply(NB, COL_G_FFN)

            def u_split(step, b):
                dve.wait_ge(act_ready, SLOTS * step + (b + 1))
                dve.sem_inc(bank_free[b], 1)
                split_weight(SLOTS * step + (AT_U + SLOTS + b), b)

            def retrieve(h, c, split):
                halves = [(k, k // 2, k % 2) for k in range(4)]
                row = lambda k: keyed[:, k, :]
                chain.did(dve.tensor_copy(keyed[:].rearrange("p (u h) n -> p u h n", u=2),
                                          scores[:, c:c + 2, ds(2 * h, 2), :]))
                chain.hold(held)
                for k, u, half in halves:
                    chain.did(dve.max(top_v[:, u, half, 0:8], row(k)))
                chain.hold(held)
                for k, u, half in halves:
                    chain.did(dve.max_index(top_i[:, u, half, 0:8], top_v[:, u, half, 0:8], row(k)))
                    chain.did(dve.match_replace(less[:, k, :], top_v[:, u, half, 0:8], row(k), LOWEST))
                split(0)
                chain.hold(held)
                for k, u, half in halves:
                    chain.did(dve.max(top_v[:, u, half, 8:16], less[:, k, :]))
                chain.hold(held)
                for k, u, half in halves:
                    chain.did(dve.max_index(top_i[:, u, half, 8:16], top_v[:, u, half, 8:16], less[:, k, :]))
                shape = [P, 2, TOPK, TOPK]
                for first, count, width, at in ((0, TOP_A, TOPK, 0), (TOP_A, TOPK - TOP_A, LOW_B, WIDE)):
                    part = [P, 2, count, width]
                    chain.did(dve.tensor_tensor(
                        cand[:, :, at:at + count * width].rearrange("p u (a b) -> p u a b", a=count),
                        top_v[:, :, 0, first:first + count].unsqueeze(3).broadcast_to(part),
                        top_v[:, :, 1, 0:width].unsqueeze(2).broadcast_to(part), ALU.add))
                split(1)
                chain.hold(held)
                unit = lambda u: top_c[:, u, :]
                for u in range(2):
                    chain.did(dve.max(unit(u)[:, 0:8], cand[:, u, :]))
                chain.hold(held)
                for u in range(2):
                    chain.did(dve.max_index(pos[:, u, 0:8], unit(u)[:, 0:8], cand[:, u, :]))
                    chain.did(dve.match_replace(cand_less[:, u, :], unit(u)[:, 0:8], cand[:, u, :], LOWEST))
                chain.hold(held)
                for u in range(2):
                    chain.did(dve.max(unit(u)[:, 8:16], cand_less[:, u, :]))
                split(2)
                chain.hold(held)
                for u in range(2):
                    chain.did(dve.max_index(pos[:, u, 8:16], unit(u)[:, 8:16], cand_less[:, u, :]))
                chain.wait()
                chain.did(dve.tensor_copy(best[:, c:c + 2, ds(h), :], top_c[:].unsqueeze(2)))
                wide_a, low_a, low_b, high_b = (place[:, k, :, :] for k in range(4))
                chain.did(dve.tensor_single_scalar(wide_a, pos[:], 4, ALU.logical_shift_right))
                chain.did(dve.tensor_single_scalar(low_a, pos[:], 2, ALU.logical_shift_right))
                chain.did(dve.tensor_single_scalar(low_b, pos[:], LOW_B - 1, ALU.bitwise_and))
                chain.did(dve.tensor_single_scalar(high_b, pos[:], TOPK - LOW_B, ALU.bitwise_and))
                chain.wait()
                chain.did(dve.scalar_tensor_tensor(rank[:, 0, :, :], low_a, float(TOP_A - WIDE // LOW_B), wide_a,
                                                   ALU.add, ALU.max))
                chain.did(dve.scalar_tensor_tensor(high_b, pos[:], float(WIDE), high_b, ALU.is_lt, ALU.mult))
                chain.wait()
                chain.did(dve.scalar_tensor_tensor(rank[:, 1, :, :], low_b, 0.0, high_b, ALU.add, ALU.add))
                chain.wait()
                for half in range(2):
                    chain.did(dve.tensor_tensor(found[:, half], rank[:, half].unsqueeze(3).broadcast_to(shape),
                                                iota_rank[:].unsqueeze(1).unsqueeze(1).broadcast_to(shape),
                                                ALU.is_equal))
                split(3)
                chain.wait()
                for half in range(2):
                    chain.did(dve.tensor_tensor(found[:, half], found[:, half],
                                                top_i[:, :, half, :].unsqueeze(2).broadcast_to(shape), ALU.mult))
                chain.wait()
                for half, to in enumerate((e1, e2)):
                    chain.did(dve.tensor_reduce(to[:, c:c + 2, ds(h), :].rearrange("p c o r -> p c (o r)"),
                                                found[:, half], AX.X, ALU.add))

            def q_split(i, b):
                dve.wait_ge(q_ready, SLOTS * i + b + 1)
                dve.sem_inc(bank_free[b], 1)
                split_weight(AT_QUERY + SLOTS * (i + 1) + b, b)

            for b in range(SLOTS):
                q_split(0, b)
            for i, (h, c) in enumerate(((0, 0), (0, 2), (1, 0)), 1):
                dve.wait_ge(scores_ready, SLOTS)
                retrieve(h, c, lambda b: q_split(i, b))
                chain.wait()
            retrieve(1, 2, lambda b: u_split(0, b))
            chain.wait()
            dve.wait_ge(scores_ready, HALVES)
            with dve.Fori(2, HEADS - 1) as h:
                chain.enter(h - 2, 2 * 47)
                for k in range(2):
                    retrieve(h, 2 * k, lambda b: u_split(2 * h + (k - 3), b))
                    chain.wait()
            chain.leave(HEADS - 3)
            retrieve(HEADS - 1, 0, lambda b: u_split(TOPK_STEPS - 2, b))
            chain.wait()

            flat = lambda tensor: tensor[:, 0, :, :].rearrange("p h r -> p (h r)")
            for k in range(2):
                chain.did(dve.scalar_tensor_tensor(expert[:, k * PAIRS:(k + 1) * PAIRS], flat(e2), float(KEYS),
                                                   flat(e1), ALU.mult, ALU.add))
            chain.wait()
            chain.did(dve.tensor_copy(expert[:, 2 * PAIRS:], expert[:, 0:ROW_SLOTS]))
            chain.did(dve.tensor_copy(row_index[:], expert[:, 0:ROW_SLOTS]))
            chain.wait()
            dve.sem_inc(rows_used, ROW_SLOTS)
            retrieve(HEADS - 1, 2, lambda b: u_split(TOPK_STEPS - 1, b))
            chain.wait()

            over_ranks = lambda tensor: tensor[:].unsqueeze(3).broadcast_to([P, CHUNKS, HEADS, TOPK])
            chain.did(dve.tensor_copy(denom[:].unsqueeze(3), best[:, :, :, 0:1]))
            chain.wait()
            dve.tensor_tensor(best[:], best[:], over_ranks(denom), ALU.subtract).then_inc(shifted, 1)

            def use_row(r, slot, times, use):
                dve.wait_ge(rows_loaded[slot], 16 * times)
                dve.tensor_copy(row_index[:, slot:slot + 1], expert[:, ds(r + ROW_SLOTS)])
                use(r, slot).then_inc(rows_used, 1)

            def dot(r, slot):
                return dve.scalar_tensor_tensor(rows[:, slot, :], rows[:, slot, :], 1.0, x_tok[:], ALU.mult, ALU.mult,
                                                accum_out=dots[:, ds(r)])

            def u_dots(s, per_pass, at, first, count):
                for k in range(first, first + count):
                    use_row(per_pass * s + (at + k), k % ROW_SLOTS,
                            per_pass // ROW_SLOTS * s + (at // ROW_SLOTS + k // ROW_SLOTS + 1), dot)

            dve.wait_ge(x_tok_ready, 2)
            for b in range(SLOTS - 1):
                u_split(TOPK_STEPS, b)
                u_dots(0, 8, 0, 2 * b, 2)
            dve.wait_ge(exp_ready, 1)
            chain.did(dve.tensor_reduce(denom[:], best[:], AX.X, ALU.add))
            chain.wait()
            chain.did(dve.reciprocal(denom[:], denom[:]))
            chain.wait()
            dve.tensor_tensor(best[:], best[:], over_ranks(denom), ALU.mult).then_inc(gates_ready, 1)
            u_split(TOPK_STEPS, SLOTS - 1)
            u_dots(0, 8, 0, 2 * (SLOTS - 1), 2)

            def gates_at_keys(s, q):
                if q >= GROUPS_PER_ROUND:
                    s, q = s + 1, q - GROUPS_PER_ROUND
                dve.wait_ge(onehots_used, GROUPS_PER_ROUND * s + (q + 1))
                for t in range(TOKENS_PER_GROUP):
                    token = ds(TOKENS_PER_ROUND * s + (TOKENS_PER_GROUP * q + t))
                    if q % 4 == 3:
                        dve.tensor_scalar(oh1[:, q % SLOTS, t, :], iota_key[:], e1_t[:, token], None,
                                          ALU.is_equal)
                    last = dve.tensor_scalar(oh2[:, q % SLOTS, t, :], iota_key[:], e2_t[:, token],
                                             gate_t[:, token], ALU.is_equal, ALU.mult)
                last.then_inc(oh2_ready, 1)

            def dve_round(s, last=False):
                for b in range(ROUND * SLOTS):
                    for q in (2 * b + 2, 2 * b + 3):
                        if not last or q < GROUPS_PER_ROUND:
                            gates_at_keys(s, q)
                    u_split(ROUND * s + (ONEHOT_AT + b // SLOTS), b % SLOTS)
                    u_dots(s, sum(ROWS_OF_ROUND), ROWS_ONEHOT, sum(ROWS_OF_ROUND[:b]), ROWS_OF_ROUND[b])

            for b in range(SLOTS):
                u_split(TOPK_STEPS + 1, b)
                if b == 2:
                    dve.wait_ge(turned_copied, 3)
                    for q in range(2):
                        gates_at_keys(0, q)
                u_dots(0, 8, 8, 2 * b, 2)

            with dve.Fori(0, ROUNDS - 1) as s:
                dve_round(s)
            dve_round(ROUNDS - 1, last=True)
            with dve.Fori(0, U_STEPS - 1 - PLAIN_AT) as s:
                for b in range(SLOTS):
                    u_split(s + PLAIN_AT, b)
                    u_dots(s, 8, ROWS_PLAIN, 2 * b, 2)

            def mask(g, b, parity):
                m = SLOTS * g + b
                if isinstance(g, int) and g < KEPT_STEPS:
                    dve.wait_ge(act_ready, SLOTS * (U_STEPS - KEPT_STEPS + g) + b + 1)
                    source = kept[:, g, b, :] if g < KEPT_STEPS - 1 else act_out[:, b, :]
                else:
                    dve.wait_ge(act_loaded[b], 16 * g + (16 - 16 * KEPT_STEPS))
                    source = act_in[:, b, :]
                if b == 0:
                    dve.wait_ge(g_loaded, 16 * g + 16)
                if b >= 2 or not isinstance(g, int) or g > 0:
                    dve.wait_ge(al_ready, m - 1)
                dve.tensor_tensor(a_f[:, b % 2, :].rearrange("p (c t) -> p c t", t=PIECE),
                                  source.rearrange("p (c t) -> p c t", t=PIECE),
                                  g_in[parity][:, :, b, :], ALU.mult).then_inc(af_ready, 1)

            def mask_lo(m, b):
                dve.wait_ge(ah_ready, m + 1)
                dve.tensor_tensor(a_lo[:, b, :], a_f[:, b % 2, :], a_hi[:, b, :].bitcast(F32), ALU.subtract
                                  ).then_inc(al_ready, 1)

            for b in range(SLOTS):
                mask(0, b, 0)
                u_split(U_STEPS - 1, b)
                mask_lo(b, b)
                u_dots(0, 8, PAIRS - 8, 2 * b, 2)

            def accumulate(r, slot):
                return dve.scalar_tensor_tensor(out_tok[:], rows[:, slot, :], dots[:, ds(r - PAIRS)], out_tok[:],
                                                ALU.mult, ALU.add)

            def v_row(g, b):
                dve.wait_ge(rows_used, ROW_SLOTS * g + (PAIRS + b))
                use_row(ROW_SLOTS * (g - 1) + (PAIRS + b), b, g + PAIRS // ROW_SLOTS, accumulate)

            dve.wait_ge(dots_gelu, 1)
            chain.did(dve.tensor_tensor(dots[:], dots[:], flat(best), ALU.mult))
            chain.did(dve.memset(out_tok[:], 0.0))
            chain.wait()

            def v_group(g, parity):
                for b in range(SLOTS):
                    mask(g, b, parity)
                    split_weight(SLOTS * g + (AT_V + b), b)
                    mask_lo(SLOTS * g + b, b)
                    v_row(g, b)

            for g in range(1, 4):
                v_group(g, g % 2)
            with dve.Fori(2, U_STEPS // 2) as i:
                for k in range(2):
                    v_group(2 * i + k, k)
            for b in range(SLOTS):
                v_row(U_STEPS, b)
            dve.wait_ge(rows_used, ROW_SLOTS + 2 * PAIRS)
            dve.sem_inc(tok_done, 1)

            for j in range(NB):
                dve.wait_ge(acc_done, j + 1)
                dve.tensor_tensor(h_t[:, j, :], bank[j][:], h_t[:, j, :], ALU.add).then_inc(h2_ready, 1)
            dve.wait_ge(summed, 2 * NB + 1)
            inverse_rms(bank[0][:])
            for j in range(NB):
                dve.scalar_tensor_tensor(out_sb[:, j, :], h_t[:, j, :],
                                         params[:, COL_G_FIN + j:COL_G_FIN + j + 1], row_stat[:],
                                         ALU.mult, ALU.mult).then_inc(out_ready, 1)


def tiles(w):
    return w.reshape(NB, P, -1, P).transpose(2, 1, 0, 3).reshape(-1, P, D)


def per_channel(v):
    return v.reshape(NB, P).T


def kernel(x, norm_mix_g, w_in, conv_w, w_conv_out, pool_w, pool_scale, w_pool_out, w_out, norm_ffn_g,
           w_query, sub_keys, expert_u, expert_v, norm_final_g):
    import concourse.bacc as bacc
    from concourse.bass_utils import run_bass_kernel_spmd

    a = {k: np.asarray(v) for k, v in locals().items() if k not in ("bacc", "run_bass_kernel_spmd")}
    w = tiles(a["w_in"][0]).reshape(6, NB, P, D)
    by_block = lambda *parts: np.stack(parts, 1).reshape(-1, P, D)
    inv_count = np.broadcast_to(1.0 / np.arange(1, PAD + 1, dtype=np.float32), (P, PAD)).astype(np.float32)
    conv_cols = a["conv_w"][0].reshape(TAPS, NB, P).transpose(2, 1, 0).reshape(P, NB * TAPS)
    pool_tiles = a["pool_w"][0].reshape(N_POOL, 2, P, 2 * P).transpose(0, 2, 1, 3).reshape(N_POOL, P, 4 * P)
    arrays = {
        "x_t": a["x"][0].T.reshape(NB, P, T).transpose(1, 0, 2),
        "params": np.concatenate([per_channel(a["norm_mix_g"][0]), per_channel(a["norm_ffn_g"][0]),
                                  per_channel(a["norm_final_g"]), per_channel(a["pool_scale"][0]),
                                  conv_cols, inv_count], 1),
        "w_in": by_block(w[3], w[1], w[2], w[0]),
        "pool": np.concatenate([pool_tiles, np.zeros_like(pool_tiles)], 2),
        "gate": by_block(w[4], w[5], tiles(a["w_conv_out"][0]), tiles(a["w_pool_out"][0])),
        "w_out": tiles(a["w_out"][0]),
        "query": tiles(a["w_query"][0]),
        "keys": a["sub_keys"][0].transpose(3, 0, 1, 2).reshape(P, HALVES, KEYS),
        "u": a["expert_u"][0].reshape(KEYS, KEYS, NB, P).transpose(1, 3, 2, 0).reshape(KEYS, P, D),
        "v": a["expert_v"][0].reshape(KEYS, KEYS, D).transpose(1, 0, 2),
        "u_rows": a["expert_u"][0].reshape(KEYS, KEYS, D).transpose(1, 0, 2),
    }
    arrays = {k: np.ascontiguousarray(v) for k, v in arrays.items()}
    nc = bacc.Bacc("TRN2", target_bir_lowering=False, num_devices=1)
    aps = [nc.dram_tensor(k, v.shape, F32, kind="ExternalInput").ap() for k, v in arrays.items()]
    out = nc.dram_tensor("out", (P, NB, T), F32, kind="ExternalOutput").ap()
    act_dram = nc.dram_tensor("act_dram", (KEYS, P, DT), F32, kind="Internal").ap()
    g_dram = nc.dram_tensor("g_dram", (P, N_PIECES, KEYS, PIECE), F32, kind="Internal").ap()
    build(nc, *aps, out, act_dram, g_dram)
    got = run_bass_kernel_spmd(nc, [arrays], core_ids=[0]).results[0]["out"]
    return np.ascontiguousarray(got.transpose(1, 0, 2).reshape(D, T).T).reshape(1, T, D)
```

```python
from contextlib import ExitStack

import numpy as np

import concourse.bass as bass
import concourse.mybir as mybir

F32, F32R, U32 = mybir.dt.float32, mybir.dt.float32r, mybir.dt.uint32
BF16 = mybir.dt.bfloat16
ALU, ACT, AX = mybir.AluOpType, mybir.ActivationFunctionType, mybir.AxisListType

P = 128
T = 512
D = 1024
NB = D // P
TAPS = 3
WINDOWS = (2, 4, 8, 16)
PAD = max(WINDOWS)
HEADS = 8
TOPK = 16
KEYS = 128
HALVES = 2 * HEADS
CHUNKS = T // P
UNITS = CHUNKS * HEADS
EPS = 1e-6
X_PARTS = 4
SLOTS = 4
LOWEST = -3.4028234663852886e38

N_IN, N_POOL = 4 * NB, len(WINDOWS)
AT_POOL = N_IN
AT_GATE = AT_POOL + N_POOL
AT_OUT = AT_GATE + 4 * NB
AT_QUERY = AT_OUT + NB
AT_U = AT_QUERY + HALVES
AT_V = AT_U + KEYS
N_TILES = AT_V + KEYS

GT = P
DT = T - GT
DENSE = slice(GT, T)
PAIRS = HEADS * TOPK
ROW_SLOTS = 4
TOP_A, LOW_B = 4, 4
WIDE = TOP_A * TOPK
CANDS = WIDE + (TOPK - TOP_A) * LOW_B

TOPK_STEPS = UNITS // 2 - 3
ONEHOT_AT = TOPK_STEPS + 2
ROUND = 2
TOKENS_PER_ROUND = 64
ROUNDS = DT // TOKENS_PER_ROUND
PLAIN_AT = ONEHOT_AT + ROUND * ROUNDS
U_STEPS = KEYS // SLOTS
TOKENS_PER_GROUP = 4
GROUPS_PER_ROUND = TOKENS_PER_ROUND // TOKENS_PER_GROUP
ACT_GROUPS = GROUPS_PER_ROUND * 3 // 4
ROWS_ONEHOT = 2 * 8
ROWS_OF_ROUND = (1, 2) * SLOTS
ROWS_PLAIN = ROWS_ONEHOT + ROUNDS * sum(ROWS_OF_ROUND)
KEPT_STEPS = 5
assert U_STEPS - KEPT_STEPS == PLAIN_AT and KEPT_STEPS == 5
PIECE = 32
N_PIECES = DT // PIECE

USES_GATE = NB
USES_OUT = USES_GATE + NB
USES_QUERY = USES_OUT + NB // SLOTS
USES_U = USES_QUERY + HALVES // SLOTS
USES_V = USES_U + U_STEPS

COL_G_MIX, COL_G_FFN, COL_G_FIN, COL_SCALE, COL_CONV = 0, 8, 16, 24, 32
COL_INV = COL_CONV + TAPS * NB
N_PARAMS = COL_INV + PAD


def ds(i, n=1):
    return bass.ds(i, n)


class MemoryMap:

    def __init__(self, nc, at):
        self.nc, self.at = nc, at

    def __call__(self, name, shape, dtype=F32):
        size = 4 * int(np.prod(shape[1:]))
        tensor = self.nc.alloc_sbuf_tensor_at(name, shape, dtype, offset=self.at)
        self.at += (size + 31) // 32 * 32
        return tensor


class Chain:

    def __init__(self, engine, sem):
        self.engine, self.sem, self.count, self.base = engine, sem, 0, 0

    def enter(self, i, per_pass):
        self.start, self.per_pass, self.count = self.base + self.count, per_pass, 0
        self.base = i * per_pass + self.start

    def leave(self, passes):
        assert self.count == self.per_pass, (self.count, self.per_pass)
        self.base, self.count = self.start + passes * self.per_pass, 0

    def did(self, instruction):
        instruction.then_inc(self.sem, 1)
        self.count += 1

    def wait(self):
        self.engine.wait_ge(self.sem, self.base + self.count)

    def hold(self, carrier):
        self.wait()
        self.engine.sem_inc(carrier, 1)


def build(nc, x_t, params_d, w_in_d, pool_d, gate_d, w_out_d, query_d, keys_d, u_d, v_d, u_rows, out_d,
          act_dram, g_dram):
    ctx = ExitStack()
    with ctx:
        fixed = MemoryMap(nc, (nc.sbuf_base + 31) // 32 * 32)
        h_t = fixed("h_t", [P, NB, T])
        w_raw = fixed("w_raw", [P, SLOTS, D])
        w_hi = fixed("w_hi", [P, SLOTS, D], F32R)
        w_lo = fixed("w_lo", [P, SLOTS, D], F32R)
        xn_at = fixed.at
        xn_hi = fixed("xn_hi", [P, NB, T], F32R)
        xn_lo = fixed("xn_lo", [P, NB, T], F32R)
        scratch = fixed("scratch", [P, 2, T])
        row_stat = fixed("row_stat", [P, T])
        stat = fixed("stat", [P, 5, CHUNKS])
        warm = fixed("warm", [P, 3])
        ones = fixed("ones", [P, P])
        ident = fixed("ident", [P, P])
        ident_r = fixed("ident_r", [P, P], F32R)
        iota_key = fixed("iota_key", [P, KEYS])
        iota_place = fixed("iota_place", [P, TOPK, TOPK], BF16)
        params = fixed("params", [P, N_PARAMS])

        front = MemoryMap(nc, fixed.at)
        u_hi = front("u_hi", [P, NB, T], F32R)
        u_lo = front("u_lo", [P, NB, T], F32R)
        mix_hi = front("mix_hi", [P, NB, T], F32R)
        mix_lo = front("mix_lo", [P, NB, T], F32R)
        in_loop = MemoryMap(nc, front.at)
        c_sb = in_loop("c_sb", [P, T])
        z_pad = in_loop("z_pad", [P, TAPS - 1 + T])
        conv = in_loop("conv", [P, 2, T])
        u_f = in_loop("u_f", [P, T])
        p_pad = in_loop("p_pad", [P, PAD + T])
        sums = in_loop("sums", [P, 2, PAD + T])
        pool_f = in_loop("pool_f", [P, T])
        edge = in_loop("edge", [P, PAD])
        mixed_f = in_loop("mixed_f", [P, T])
        gate_loop = MemoryMap(nc, front.at)
        merged_hi = gate_loop("merged_hi", [P, NB, T], F32R)
        merged_lo = gate_loop("merged_lo", [P, NB, T], F32R)
        sig_a = gate_loop("sig_a", [P, T])
        sig_b = gate_loop("sig_b", [P, T])

        peer = MemoryMap(nc, fixed.at)
        keys_t = peer("keys_t", [P, HALVES, KEYS])
        q_sb = peer("q_sb", [P, SLOTS, T])
        scores = peer("scores", [P, CHUNKS, HALVES, KEYS])
        rest = MemoryMap(nc, peer.at)
        act_out = rest("act_out", [P, SLOTS, DT])
        e1_t = rest("e1_t", [P, DT])
        e2_t = rest("e2_t", [P, DT])
        gate_t = rest("gate_t", [P, DT])
        best = rest("best", [P, CHUNKS, HEADS, TOPK])
        e1 = rest("e1", [P, CHUNKS, HEADS, TOPK])
        e2 = rest("e2", [P, CHUNKS, HEADS, TOPK])
        denom = rest("denom", [P, CHUNKS, HEADS])
        expert = rest("expert", [P, 2 * PAIRS + ROW_SLOTS], U32)
        row_index = rest("row_index", [P, ROW_SLOTS], U32)
        rows = rest("rows", [P, ROW_SLOTS, D])
        x_tok = rest("x_tok", [P, D])
        after_topk = MemoryMap(nc, rest.at)
        out_tok = after_topk("out_tok", [P, D])
        dots = after_topk("dots", [P, PAIRS])
        kept = after_topk("kept", [P, 2, SLOTS, DT])
        top_v = rest("top_v", [P, 2, 2, TOPK])
        top_i = rest("top_i", [P, 2, 2, TOPK], U32)
        less = rest("less", [P, 4, KEYS])
        cand = rest("cand", [P, 2, CANDS])
        cand_less = rest("cand_less", [P, 2, CANDS])
        keyed = rest("keyed", [P, 4, KEYS])
        top_c = rest("top_c", [P, 2, TOPK])
        pos = rest("pos", [P, 2, TOPK], U32)
        rank = rest("rank", [P, 2, 2, TOPK], BF16)
        parts = rest("parts", [P, 4, 2, TOPK], U32)
        found = rest("found", [P, 2, 2, TOPK, TOPK], BF16)
        assert max(rest.at, after_topk.at) <= nc.sbuf_usable_end and gate_loop.at <= nc.sbuf_usable_end
        g_build = MemoryMap(nc, fixed.at)
        oh1 = g_build("oh1", [P, SLOTS, TOKENS_PER_GROUP, KEYS])
        oh2 = g_build("oh2", [P, SLOTS, TOKENS_PER_GROUP, KEYS])
        g_sb = g_build("g_sb", [P, 2, KEYS, PIECE])
        assert g_build.at <= peer.at
        v_part = MemoryMap(nc, fixed.at)
        act_in = v_part("act_in", [P, SLOTS, DT])
        g_in = [region(f"g_in{k}", [P, N_PIECES, SLOTS, PIECE])
                for k, region in enumerate((v_part, MemoryMap(nc, xn_at)))]
        a_f = v_part("a_f", [P, 2, DT])
        a_hi = v_part("a_hi", [P, SLOTS, DT], F32R)
        a_lo = v_part("a_lo", [P, SLOTS, DT], F32R)
        assert v_part.at <= peer.at
        def kept_at(k, b):
            if k == 0:
                return act_in[:, b, :]
            if k == 1:
                return (e1_t[:], e2_t[:], gate_t[:], e1[:].rearrange("p c h r -> p (c h r)")[:, 0:DT])[b]
            if k < KEPT_STEPS - 1:
                return kept[:, k - 2, b, :]
            return act_out[:, b, :]

        squares = MemoryMap(nc, xn_at)("squares", [P, NB, T])
        out_sb = MemoryMap(nc, fixed.at)("out_sb", [P, NB, T])

        bank = [ctx.enter_context(nc.psum_tensor(f"bank{b}", [P, T], F32)) for b in range(8)]

        def sem(name):
            return ctx.enter_context(nc.semaphore(name))

        x_loaded = [sem(f"x_loaded{k}") for k in range(X_PARTS)]
        params_loaded = sem("params_loaded")
        keys_loaded = sem("keys_loaded")
        raw_loaded = [sem(f"raw_loaded{k}") for k in range(SLOTS)]
        hi_done = sem("hi_done")
        lo_done = sem("lo_done")
        job_done = sem("job_done")
        bank_free = [sem(f"bank_free{b}") for b in range(SLOTS)]
        consts = sem("consts")
        squared = sem("squared")
        added = sem("added")
        summed = sem("summed")
        h_ready = sem("h_ready")
        xn_f = sem("xn_f")
        xn_h = sem("xn_h")
        xn_l = sem("xn_l")
        c_copied, p_copied = sem("c_copied"), sem("p_copied")
        uf_ready, uh_ready, ul_ready = sem("uf_ready"), sem("uh_ready"), sem("ul_ready")
        pf_ready, ph_ready, pl_ready = sem("pf_ready"), sem("ph_ready"), sem("pl_ready")
        mf_ready, mh_ready, ml_ready = sem("mf_ready"), sem("mh_ready"), sem("ml_ready")
        sigmoids = sem("sigmoids")
        gf_ready, gh_ready, gl_ready = sem("gf_ready"), sem("gh_ready"), sem("gl_ready")
        q_ready, scored, scores_ready = sem("q_ready"), sem("scored"), sem("scores_ready")
        act_ready = sem("act_ready")
        act_stored = [sem(f"act_stored{b}") for b in range(SLOTS)]
        shifted, exp_ready, gates_ready = sem("shifted"), sem("exp_ready"), sem("gates_ready")
        turned, turned_copied = sem("turned"), sem("turned_copied")
        gaps_ready = sem("gaps_ready")
        oh1_ready = sem("oh1_ready")
        oh2_ready = sem("oh2_ready")
        onehots_used = sem("onehots_used")
        g_copied = sem("g_copied")
        g_stored = [sem(f"g_stored{k}") for k in range(2)]
        act_loaded = [sem(f"act_loaded{b}") for b in range(SLOTS)]
        g_loaded = sem("g_loaded")
        af_ready, ah_ready, al_ready = sem("af_ready"), sem("ah_ready"), sem("al_ready")
        acc_done = sem("acc_done")
        h2_ready, out_ready, out_stored = sem("h2_ready"), sem("out_ready"), sem("out_stored")
        ident_ready = sem("ident_ready")
        x_turned, x_tok_ready = sem("x_turned"), sem("x_tok_ready")
        rows_loaded = [sem(f"rows_loaded{k}") for k in range(ROW_SLOTS)]
        wait_carried = sem("wait_carried")
        rows_used = sem("rows_used")
        dots_gelu = sem("dots_gelu")
        tok_done = sem("tok_done")
        var_ready, root_ready = sem("var_ready"), sem("root_ready")
        diag_ready = sem("diag_ready")
        spread = sem("spread")
        warmed = sem("warmed")
        held = sem("held")
        dve_step = sem("dve_step")

        block = ctx.enter_context(nc.Block())

        @block.sync
        def _(sp):
            def load_raw(source, k, n, slot):
                if not isinstance(n, int) or n >= SLOTS:
                    sp.wait_ge(lo_done, n - SLOTS + 1)
                sp.dma_start(w_raw[:, slot, :], source[ds(k), :, :].rearrange("o p d -> (o p) d")
                             ).then_inc(raw_loaded[slot], 16)

            def load_all(source, first, count, start=0):
                with sp.Fori(start // SLOTS, count // SLOTS) as i:
                    for b in range(SLOTS):
                        load_raw(source, SLOTS * i + b, SLOTS * i + (first + b), b)

            for k in range(X_PARTS):
                blocks = slice(k * NB // X_PARTS, (k + 1) * NB // X_PARTS)
                sp.dma_start(h_t[:, blocks, :], x_t[:, blocks, :]).then_inc(x_loaded[k], 16)
            sp.dma_start(params[:], params_d).then_inc(params_loaded, 16)
            for b in range(SLOTS):
                load_raw(w_in_d, b, b, b)
            load_all(w_in_d, 0, N_IN, start=SLOTS)
            load_all(pool_d, AT_POOL, N_POOL)
            load_all(gate_d, AT_GATE, 4 * NB)
            load_all(w_out_d, AT_OUT, NB)
            for k in range(HALVES):
                if k == 2 * SLOTS:
                    sp.wait_ge(job_done, AT_QUERY)
                    sp.dma_start(keys_t[:], keys_d).then_inc(keys_loaded, 16)
                load_raw(query_d, k, AT_QUERY + k, k % SLOTS)
            load_all(u_d, AT_U, KEYS)

            for k in range(2):
                sp.wait_ge(g_stored[k], 16 * N_PIECES // 2)

            def load_v_group(g, parity):
                if isinstance(g, int):
                    e2 = SLOTS * (g - KEPT_STEPS) % KEYS
                else:
                    e2 = SLOTS * (g - KEPT_STEPS)
                for b in range(SLOTS):
                    load_raw(v_d, e2 + b, SLOTS * g + (AT_V + b), b)
                    if not isinstance(g, int) or g >= KEPT_STEPS:
                        sp.wait_ge(af_ready, b + 1 if isinstance(g, int) and g == KEPT_STEPS else
                                   SLOTS * g + (b - SLOTS + 1))
                        sp.wait_ge(act_stored[b], 16 * g + (16 - 16 * KEPT_STEPS))
                        sp.dma_start(act_in[:, b, :],
                                     act_dram[ds(e2 + b), :, :].rearrange("o p t -> (o p) t")
                                     ).then_inc(act_loaded[b], 16)
                    if b == 0:
                        if not isinstance(g, int) or g >= 2:
                            sp.wait_ge(af_ready, SLOTS * g - SLOTS)
                        elif g == 1:
                            sp.wait_ge(job_done, AT_V)
                        sp.dma_start(g_in[parity][:], g_dram[:, :, ds(e2, SLOTS), :]).then_inc(g_loaded, 16)

            for g in range(KEPT_STEPS + 1):
                load_v_group(g, g % 2)
            with sp.Fori((KEPT_STEPS + 1) // 2, U_STEPS // 2) as i:
                for k in range(2):
                    load_v_group(2 * i + k, k)

            for j in range(NB):
                sp.wait_ge(out_ready, j + 1)
                sp.dma_start(out_d[:, j, :], out_sb[:, j, :]).then_inc(out_stored, 16)
            sp.wait_ge(out_stored, 16 * NB)

        @block.gpsimd
        def _(pool):
            pool.memset(ones[:], 1.0).then_inc(consts, 1)
            pool.memset(z_pad[:, 0:TAPS - 1], 0.0).then_inc(consts, 1)
            pool.memset(p_pad[:, 0:PAD], 0.0).then_inc(consts, 1)
            pool.memset(ident[:], 0.0).then_inc(consts, 1)
            pool.iota(iota_place[:], pattern=[[1, TOPK], [0, TOPK]], base=0, channel_multiplier=0,
                      allow_small_or_imprecise_dtypes=True).then_inc(consts, 1)
            pool.iota(iota_key[:], pattern=[[1, KEYS]], base=0, channel_multiplier=0,
                      allow_small_or_imprecise_dtypes=True).then_inc(consts, 1)
            pool.wait_ge(consts, 6)
            pool.affine_select(out=ident[:], in_=ident[:], compare_op=ALU.not_equal, fill=1.0, base=0,
                               pattern=[[-1, P]], channel_multiplier=1).then_inc(consts, 1)

            def gather(table, r, slot):
                pool.wait_ge(rows_used, r + 1)
                pool.sem_inc(wait_carried, 1)
                pool.indirect_dma_start(out=rows[:, slot, :], out_offset=None,
                                        in_=table.rearrange("a p d -> (a p) d"),
                                        in_offset=bass.IndirectOffsetOnAxis(ap=row_index[:, slot:slot + 1], axis=0)
                                        ).then_inc(rows_loaded[slot], 16)

            for table, at in ((u_rows, 0), (v_d, PAIRS)):
                with pool.Fori(0, PAIRS // ROW_SLOTS) as g:
                    for slot in range(ROW_SLOTS):
                        gather(table, ROW_SLOTS * g + (at + slot), slot)

        @block.scalar
        def _(act):
            def load_root_table(count):
                act.activation(warm[:, count - 1:count], ones[:, 0:1], ACT.Sqrt).then_inc(warmed, 1)

            def root(count):
                act.wait_ge(var_ready, count)
                act.activation(stat[:, 1, :], stat[:, 0, :], ACT.Sqrt).then_inc(root_ready, 1)

            def split_weight(n, slot, times):
                act.wait_ge(raw_loaded[slot], 16 * times)
                if not isinstance(n, int) or n >= SLOTS:
                    act.wait_ge(job_done, n - SLOTS + 1)
                act.activation(w_hi[:, slot, :], w_raw[:, slot, :], ACT.Copy).then_inc(hi_done, 1)

            def norm_hi(base):
                for j in range(NB):
                    act.wait_ge(xn_f, base + j + 1)
                    act.activation(xn_hi[:, j, :], scratch[:, j % 2, :], ACT.Copy).then_inc(xn_h, 1)

            act.wait_ge(consts, 1)
            load_root_table(1)
            for j in range(NB):
                if j % (NB // X_PARTS) == 0:
                    act.wait_ge(x_loaded[j * X_PARTS // NB], 16)
                act.activation(squares[:, j, :], h_t[:, j, :], ACT.Square).then_inc(squared, 1)
            split_weight(0, 0, 1)
            root(1)
            split_weight(1, 1, 1)
            norm_hi(0)
            split_weight(2, 2, 1)
            split_weight(3, 3, 1)

            with act.Fori(0, NB) as i:
                act.wait_ge(job_done, SLOTS * i + 1)
                act.activation(p_pad[:, PAD:], bank[0][:], ACT.Copy).then_inc(p_copied, 1)
                split_weight(SLOTS * i + 4, 0, i + 2)
                act.wait_ge(job_done, SLOTS * i + 2)
                act.activation(c_sb[:], bank[1][:], ACT.Copy).then_inc(c_copied, 1)
                split_weight(SLOTS * i + 5, 1, i + 2)
                act.wait_ge(pf_ready, i + 1)
                act.activation(mix_hi[:, ds(i), :], pool_f[:], ACT.Copy).then_inc(ph_ready, 1)
                split_weight(SLOTS * i + 6, 2, i + 2)
                split_weight(SLOTS * i + 7, 3, i + 2)
                act.wait_ge(uf_ready, i + 1)
                act.activation(u_hi[:, ds(i), :], u_f[:], ACT.Copy).then_inc(uh_ready, 1)

            for g in range(N_POOL):
                act.wait_ge(job_done, AT_POOL + g + 1)
                for jo in range(2):
                    j = 2 * g + jo
                    if j >= 1:
                        act.wait_ge(ml_ready, j)
                    act.activation(mixed_f[:], bank[4 + 2 * (g % 2) + jo][:], ACT.Copy,
                                   scale=params[:, COL_SCALE + j:COL_SCALE + j + 1]).then_inc(mf_ready, 1)
                    act.wait_ge(mf_ready, j + 1)
                    act.activation(mix_hi[:, j, :], mixed_f[:], ACT.Copy).then_inc(mh_ready, 1)
                split_weight(AT_GATE + g, g, NB + 2)

            with act.Fori(0, NB) as i:
                for b, sig in ((0, sig_a), (1, sig_b)):
                    act.wait_ge(job_done, SLOTS * i + (AT_GATE + b + 1))
                    act.activation(sig[:], bank[b][:], ACT.Sigmoid).then_inc(sigmoids, 1)
                    split_weight(SLOTS * i + (AT_GATE + SLOTS + b), b, i + (NB + 3))
                for b in (2, 3):
                    split_weight(SLOTS * i + (AT_GATE + SLOTS + b), b, i + (NB + 3))
                act.wait_ge(gf_ready, i + 1)
                act.activation(merged_hi[:, ds(i), :], scratch[:, 0, :], ACT.Copy).then_inc(gh_ready, 1)

            load_root_table(2)
            with act.Fori(0, NB // SLOTS) as i:
                for b in range(SLOTS):
                    split_weight(SLOTS * i + (AT_OUT + SLOTS + b), b, i + (2 * NB + 3))
                    act.wait_ge(h_ready, SLOTS * i + (b + 1))
                    act.activation(scratch[:, b % 2, :], h_t[:, ds(SLOTS * i + b), :], ACT.Square).then_inc(squared, 1)
            root(2)
            norm_hi(NB)

            with act.Fori(0, HALVES // SLOTS) as i:
                def copy_scores(b):
                    act.wait_ge(scored, SLOTS * i + (b + 1))
                    act.activation(scores[:, :, ds(SLOTS * i + b), :].rearrange("p c o n -> p c (o n)"),
                                   bank[4 + b][:].rearrange("p (c n) -> p c n", c=CHUNKS),
                                   ACT.Copy).then_inc(scores_ready, 1)

                for b in range(SLOTS):
                    act.wait_ge(job_done, SLOTS * i + (AT_QUERY + b + 1))
                    act.activation(q_sb[:, b, :], bank[b][:], ACT.Copy).then_inc(q_ready, 1)
                    split_weight(SLOTS * i + (AT_QUERY + SLOTS + b), b, i + (AT_QUERY // SLOTS + 2))
                    if b >= 1:
                        copy_scores(b - 1)
                copy_scores(SLOTS - 1)

            for k in range(2):
                act.wait_ge(x_turned, k + 1)
                act.activation(x_tok[:, k * T:(k + 1) * T], bank[4 + k][:], ACT.Copy).then_inc(x_tok_ready, 1)

            def gelu_tile(step, b):
                act.wait_ge(job_done, SLOTS * step + (AT_U + b + 1))
                stored = not isinstance(step, int) or step < U_STEPS - KEPT_STEPS
                to = act_out[:, b, :]
                if not isinstance(step, int) or 0 < step < U_STEPS - KEPT_STEPS:
                    act.wait_ge(act_stored[b], 16 * step)
                elif step == U_STEPS - 1:
                    act.wait_ge(act_stored[b], 16 * (U_STEPS - KEPT_STEPS))
                elif not stored:
                    to = kept_at(step - (U_STEPS - KEPT_STEPS), b)
                act.activation(to, bank[b][:, DENSE], ACT.Gelu).then_inc(act_ready, 1)
                split_weight(SLOTS * step + (AT_U + SLOTS + b), b, step + (AT_U // SLOTS + 2))
                if stored:
                    act.wait_ge(act_ready, SLOTS * step + (b + 1))
                    act.dma_start(act_dram[ds(SLOTS * step + b), :, :].rearrange("o p t -> (o p) t"),
                                  act_out[:, b, :]).then_inc(act_stored[b], 16)

            key_gap = lambda q: scratch[:, q % 2, :].rearrange("p (t n) -> p t n", n=KEYS)

            def one_hots(s, q):
                if q >= GROUPS_PER_ROUND:
                    s, q = s + 1, q - GROUPS_PER_ROUND
                if q % 4 == 3:
                    return
                n = ACT_GROUPS * s + (q - q // 4)
                gap = key_gap(q - q // 4)
                act.wait_ge(onehots_used, GROUPS_PER_ROUND * s + (q + 1))
                if not isinstance(n, int) or n >= 2:
                    act.wait_ge(oh1_ready, n - 1)
                for t in range(TOKENS_PER_GROUP):
                    last = act.activation(gap[:, t, :], iota_key[:], ACT.Abs, scale=-1.0,
                                          bias=e1_t[:, ds(TOKENS_PER_ROUND * s + (TOKENS_PER_GROUP * q + t))])
                last.then_inc(gaps_ready, 1)
                act.wait_ge(gaps_ready, n + 1)
                act.activation(oh1[:, q % SLOTS, :, :], gap, ACT.Relu, scale=-1.0,
                               bias=ones[:, 0:1]).then_inc(oh1_ready, 1)

            def copy_g(s, q):
                k, t = q // 8, TOKENS_PER_GROUP * (q % 8)
                if q % 8 == 0 and (not isinstance(s, int) or s > 0):
                    act.wait_ge(g_stored[k], 16 * s)
                act.wait_ge(onehots_used, GROUPS_PER_ROUND * s + (SLOTS + q + 1))
                act.activation(g_sb[:, k, :, t:t + TOKENS_PER_GROUP].rearrange("p e t -> p t e"),
                               bank[4 + q % SLOTS][:].rearrange("p (t e) -> p t e", e=KEYS),
                               ACT.Copy).then_inc(g_copied, 1)

            def store_g(s, k):
                act.wait_ge(g_copied, GROUPS_PER_ROUND * s + (SLOTS + 8 * (k + 1)))
                act.dma_start(g_dram[:, ds(2 * s + k), :, :].rearrange("p o e t -> p (o e) t"),
                              g_sb[:, k, :, :]).then_inc(g_stored[k], 16)

            def g_round(s, last=False):
                for b in range(ROUND * SLOTS):
                    gelu_tile(ROUND * s + (ONEHOT_AT + b // SLOTS), b % SLOTS)
                    for q in (2 * b, 2 * b + 1):
                        if not last or q + 2 < GROUPS_PER_ROUND:
                            one_hots(s, q + 2)
                        copy_g(s, q)
                    if b % SLOTS == SLOTS - 1:
                        store_g(s, b // SLOTS)

            for b in range(SLOTS):
                gelu_tile(0, b)
            with act.Fori(1, TOPK_STEPS) as step:
                for b in range(SLOTS):
                    gelu_tile(step, b)
            for b in range(SLOTS // 2):
                gelu_tile(TOPK_STEPS, b)
            act.wait_ge(shifted, 1)
            act.activation(best[:], best[:], ACT.Exp).then_inc(exp_ready, 1)
            for b in range(SLOTS // 2, SLOTS):
                gelu_tile(TOPK_STEPS, b)
            for b in range(SLOTS // 2):
                gelu_tile(TOPK_STEPS + 1, b)
            for k, turned_to in enumerate((e1_t, e2_t, gate_t)):
                act.wait_ge(turned, k + 1)
                act.activation(turned_to[:], bank[4 + k][:, 0:DT], ACT.Copy).then_inc(turned_copied, 1)
            act.sem_inc(g_copied, SLOTS)
            act.wait_ge(turned_copied, 1)
            for b in range(SLOTS // 2, SLOTS):
                gelu_tile(TOPK_STEPS + 1, b)
                one_hots(0, b - SLOTS // 2)
            g_round(0)
            with act.Fori(1, ROUNDS - 1) as s:
                g_round(s)
            g_round(ROUNDS - 1, last=True)
            for step in range(U_STEPS - KEPT_STEPS, U_STEPS - 1):
                for b in range(SLOTS):
                    gelu_tile(step, b)

            def split_a(m, b):
                act.wait_ge(af_ready, m + 1)
                act.activation(a_hi[:, b, :], a_f[:, b % 2, :], ACT.Copy).then_inc(ah_ready, 1)

            for b in range(SLOTS):
                gelu_tile(U_STEPS - 1, b)
                split_a(b, b)
            def v_group(g):
                for b in range(SLOTS):
                    split_weight(SLOTS * g + (AT_V + b), b, g + (AT_V // SLOTS + 1))
                    split_a(SLOTS * g + b, b)

            v_group(1)
            act.wait_ge(rows_used, ROW_SLOTS + PAIRS)
            act.activation(dots[:], dots[:], ACT.Gelu).then_inc(dots_gelu, 1)
            with act.Fori(2, U_STEPS) as g:
                v_group(g)

            load_root_table(3)
            for j in range(NB):
                act.wait_ge(h2_ready, j + 1)
                act.activation(squares[:, j, :], h_t[:, j, :], ACT.Square).then_inc(squared, 1)
            root(3)

        @block.tensor
        def _(pe):
            def k_block(tensor, slot, k):
                return tensor[:, slot, k * P:(k + 1) * P]

            def tile_product(n, b, uses, act_hi, act_lo, parts=None, base=0, tokens=slice(0, T)):
                pe.wait_ge(lo_done, n + 1)
                pe.wait_ge(bank_free[b], uses)
                for k in range(NB):
                    if parts is not None:
                        pe.wait_ge(parts, base + k + 1)
                    hi, lo = k_block(w_hi, b, k), k_block(w_lo, b, k)
                    out = bank[b][:, tokens]
                    pe.matmul(out, hi, act_hi[:, k, tokens], start=k == 0, stop=False)
                    pe.matmul(out, hi, act_lo[:, k, tokens], start=False, stop=False)
                    last = pe.matmul(out, lo, act_hi[:, k, tokens], start=False, stop=k == NB - 1)
                last.then_inc(job_done, 1)

            def sum_squares(to, source, j):
                for c in range(CHUNKS):
                    last = pe.matmul(bank[to][:, c * NB + j:c * NB + j + 1], source[:, c * P:(c + 1) * P],
                                     ones[:, 0:1], start=True, stop=True)
                last.then_inc(summed, 1)

            def spread_inverse(to, count):
                pe.wait_ge(diag_ready, count)
                pe.matmul(bank[to][:], ones[:], row_stat[:], start=True, stop=True).then_inc(spread, 1)

            pe.wait_ge(consts, 7)
            pe.wait_ge(added, 1)
            sum_squares(4, squares[:, 0, :], 0)
            spread_inverse(5, 1)

            with pe.Fori(0, NB) as i:
                for b in range(SLOTS):
                    tile_product(SLOTS * i + b, b, i + 1, xn_hi, xn_lo, xn_l if b == 0 else None)

            pe.wait_ge(pl_ready, NB)
            for g in range(N_POOL):
                pe.wait_ge(lo_done, AT_POOL + g + 1)
                if g >= 2:
                    pe.wait_ge(mf_ready, 2 * (g - 1))
                for jo in range(2):
                    to = bank[4 + 2 * (g % 2) + jo]
                    for ki in range(2):
                        hi, lo = k_block(w_hi, g, 2 * ki + jo), k_block(w_lo, g, 2 * ki + jo)
                        x_hi, x_lo = mix_hi[:, 2 * g + ki, :], mix_lo[:, 2 * g + ki, :]
                        pe.matmul(to[:], hi, x_hi, start=ki == 0, stop=False)
                        pe.matmul(to[:], hi, x_lo, start=False, stop=False)
                        last = pe.matmul(to[:], lo, x_hi, start=False, stop=ki == 1)
                last.then_inc(job_done, 1)

            with pe.Fori(0, NB) as i:
                for b, (a_h, a_l) in enumerate(((xn_hi, xn_lo), (xn_hi, xn_lo), (u_hi, u_lo), (mix_hi, mix_lo))):
                    if b == 2:
                        pe.wait_ge(ul_ready, NB)
                        pe.wait_ge(ml_ready, NB)
                    tile_product(SLOTS * i + (AT_GATE + b), b, i + (USES_GATE + 1), a_h, a_l)

            with pe.Fori(0, NB // SLOTS) as i:
                for b in range(SLOTS):
                    tile_product(SLOTS * i + (AT_OUT + b), b, i + (USES_OUT + 1), merged_hi, merged_lo,
                                 gl_ready if b == 0 else None)
            pe.wait_ge(h_ready, NB + 1)
            sum_squares(4, row_stat, 0)
            spread_inverse(5, 2)

            pe.wait_ge(keys_loaded, 16)
            with pe.Fori(0, HALVES // SLOTS) as i:
                def score(b):
                    pe.wait_ge(q_ready, SLOTS * i + (b + 1))
                    for c in range(CHUNKS):
                        last = pe.matmul(bank[4 + b][:, c * KEYS:(c + 1) * KEYS], q_sb[:, b, c * P:(c + 1) * P],
                                         keys_t[:, ds(SLOTS * i + b), :].rearrange("p o n -> p (o n)"),
                                         start=True, stop=True)
                    last.then_inc(scored, 1)

                for b in range(SLOTS):
                    tile_product(SLOTS * i + (AT_QUERY + b), b, i + (USES_QUERY + 1), xn_hi, xn_lo,
                                 xn_l if b == 0 else None, NB)
                    if b >= 1:
                        score(b - 1)
                score(SLOTS - 1)

            pe.wait_ge(scores_ready, HALVES)
            pe.wait_ge(ident_ready, 1)
            for k in range(2):
                for j in range(4 * k, 4 * k + 4):
                    at = bank[4 + k][:, (j - 4 * k) * P:(j - 4 * k + 1) * P]
                    pe.matmul(at, xn_hi[:, j, 0:GT], ident_r[:], start=True, stop=False)
                    last = pe.matmul(at, xn_lo[:, j, 0:GT], ident_r[:], start=False, stop=True)
                last.then_inc(x_turned, 1)

            def u_tile(step, b):
                tile_product(SLOTS * step + (AT_U + b), b, step + (USES_U + 1), xn_hi, xn_lo, tokens=DENSE)

            with pe.Fori(0, ONEHOT_AT - 1) as step:
                for b in range(SLOTS):
                    u_tile(step, b)
            for b in range(SLOTS // 2):
                u_tile(ONEHOT_AT - 1, b)
            pe.wait_ge(x_tok_ready, 2)
            pe.wait_ge(gates_ready, 1)
            for k, tensor in enumerate((e1, e2, best)):
                for c in range(1, CHUNKS):
                    last = pe.transpose(bank[4 + k][:, (c - 1) * P:c * P],
                                        tensor[:, c, :, :].rearrange("p h r -> p (h r)"), ident[:])
                last.then_inc(turned, 1)
            for b in range(SLOTS // 2, SLOTS):
                u_tile(ONEHOT_AT - 1, b)

            pe.sem_inc(onehots_used, SLOTS)
            with pe.Fori(0, ROUNDS) as s:
                for b in range(ROUND * SLOTS):
                    u_tile(ROUND * s + (ONEHOT_AT + b // SLOTS), b % SLOTS)
                    for q in (2 * b, 2 * b + 1):
                        if q % 4 != 3:
                            pe.wait_ge(oh1_ready, ACT_GROUPS * s + (q - q // 4 + 1))
                        pe.wait_ge(oh2_ready, GROUPS_PER_ROUND * s + (q + 1))
                        pe.wait_ge(g_copied, GROUPS_PER_ROUND * s + (q + 1))
                        for t in range(TOKENS_PER_GROUP):
                            last = pe.matmul(bank[4 + q % SLOTS][:, t * KEYS:(t + 1) * KEYS],
                                             oh1[:, q % SLOTS, t, :], oh2[:, q % SLOTS, t, :],
                                             start=True, stop=True)
                        last.then_inc(onehots_used, 1)
            with pe.Fori(PLAIN_AT, U_STEPS) as step:
                for b in range(SLOTS):
                    u_tile(step, b)

            def v_tile(g, b, first=False, final=False):
                pe.wait_ge(lo_done, SLOTS * g + (AT_V + b + 1))
                pe.wait_ge(al_ready, SLOTS * g + (b + 1))
                for j in range(NB):
                    if first and j < SLOTS:
                        pe.wait_ge(bank_free[j], USES_V + 1)
                    hi, lo = k_block(w_hi, b, j), k_block(w_lo, b, j)
                    out = bank[j][:, DENSE]
                    pe.matmul(out, hi, a_hi[:, b, :], start=first, stop=False)
                    pe.matmul(out, hi, a_lo[:, b, :], start=False, stop=False)
                    last = pe.matmul(out, lo, a_hi[:, b, :], start=False, stop=final)
                last.then_inc(job_done, 1)

            pe.wait_ge(g_copied, SLOTS + DT // TOKENS_PER_GROUP)
            for b in range(SLOTS):
                v_tile(0, b, first=b == 0)
            with pe.Fori(1, U_STEPS - 1) as g:
                for b in range(SLOTS):
                    v_tile(g, b)
            for b in range(SLOTS):
                v_tile(U_STEPS - 1, b, final=b == SLOTS - 1)

            pe.wait_ge(tok_done, 1)
            for j in range(NB):
                pe.transpose(bank[j][:, 0:GT], out_tok[:, j * P:(j + 1) * P], ident[:]).then_inc(acc_done, 1)

            for j in range(NB // 2):
                pe.wait_ge(added, 1 + j + 1)
                sum_squares(0, squares[:, 2 * j, :], j)
            spread_inverse(1, 3)

        @block.vector
        def _(dve):
            chain = Chain(dve, dve_step)
            norms = [0]

            def split_weight(n, slot):
                dve.wait_ge(hi_done, n + 1)
                dve.tensor_tensor(w_lo[:, slot, :], w_raw[:, slot, :], w_hi[:, slot, :].bitcast(F32),
                                  ALU.subtract).then_inc(lo_done, 1)

            def inverse_rms(sums, columns):
                norms[0] += 1
                var, rt, y, t, total = (stat[:, k, :] for k in range(5))
                sums = sums[:, 0:CHUNKS * NB].rearrange("p (c j) -> p c j", j=NB)[:, :, 0:columns]
                chain.did(dve.tensor_reduce(total, sums, AX.X, ALU.add))
                chain.wait()
                dve.tensor_scalar(var, total, 1.0 / D, EPS, ALU.mult, ALU.add).then_inc(var_ready, 1)
                dve.wait_ge(root_ready, norms[0])
                chain.did(dve.reciprocal(y, rt))
                chain.wait()
                chain.did(dve.tensor_tensor(t, y, y, ALU.mult))
                chain.wait()
                chain.did(dve.tensor_tensor(t, t, var, ALU.mult))
                chain.wait()
                chain.did(dve.tensor_scalar(t, t, -0.5, 1.5, ALU.mult, ALU.add))
                chain.wait()
                chain.did(dve.tensor_tensor(t, y, t, ALU.mult))
                chain.wait()
                diagonal = [P, CHUNKS, P]
                dve.tensor_tensor(row_stat[:].rearrange("p (c t) -> p c t", c=CHUNKS),
                                  ident[:].unsqueeze(1).broadcast_to(diagonal),
                                  t.unsqueeze(2).broadcast_to(diagonal), ALU.mult).then_inc(diag_ready, 1)
                dve.wait_ge(spread, norms[0])

            def norm_apply(base, gain_col):
                def lo(j):
                    dve.wait_ge(xn_h, base + j + 1)
                    dve.tensor_tensor(xn_lo[:, j, :], scratch[:, j % 2, :], xn_hi[:, j, :].bitcast(F32),
                                      ALU.subtract).then_inc(xn_l, 1)

                for j in range(NB):
                    if j >= 2:
                        dve.wait_ge(xn_l, base + j - 1)
                    dve.scalar_tensor_tensor(scratch[:, j % 2, :], h_t[:, j, :],
                                             params[:, gain_col + j:gain_col + j + 1], bank[5][:],
                                             ALU.mult, ALU.mult).then_inc(xn_f, 1)
                    if j >= 1:
                        lo(j - 1)
                lo(NB - 1)

            for b in range(SLOTS):
                dve.sem_inc(bank_free[b], 1)
            for j in range(1, NB):
                dve.wait_ge(squared, j + 1)
                chain.wait()
                add = dve.tensor_tensor(squares[:, 0, :], squares[:, 0, :], squares[:, j, :], ALU.add)
                if j < NB - 1:
                    chain.did(add)
                else:
                    add.then_inc(added, 1)
            split_weight(0, 0)
            dve.wait_ge(params_loaded, 16)
            dve.wait_ge(consts, 7)
            dve.wait_ge(summed, 1)
            inverse_rms(bank[4], 1)
            norm_apply(0, COL_G_MIX)
            for b in range(1, SLOTS):
                split_weight(b, b)
            dve.wait_ge(consts, 7)
            dve.tensor_copy(ident_r[:], ident[:]).then_inc(ident_ready, 1)

            def in_block(i, window):
                tap = lambda k: params[:, ds(TAPS * i + (COL_CONV + k))]
                dve.wait_ge(p_copied, i + 1)
                dve.sem_inc(bank_free[0], 1)
                source, width, side = p_pad[:], 1, 0
                while width < window:
                    begin = 2 * width - 1
                    chain.did(dve.tensor_tensor(sums[:, side, begin:], source[:, begin:],
                                                source[:, begin - width:PAD + T - width], ALU.add))
                    chain.wait()
                    source, width, side = sums[:, side, :], 2 * width, 1 - side
                chain.did(dve.tensor_tensor(edge[:, 0:window], source[:, PAD:PAD + window],
                                            params[:, COL_INV:COL_INV + window], ALU.mult))
                chain.did(dve.scalar_tensor_tensor(pool_f[:], source[:, PAD:], 1.0 / window, p_pad[:, PAD:],
                                                   ALU.mult, ALU.subtract))
                chain.wait()
                dve.tensor_tensor(pool_f[:, 0:window], edge[:, 0:window], p_pad[:, PAD:PAD + window],
                                  ALU.subtract).then_inc(pf_ready, 1)
                split_weight(SLOTS * i + 4, 0)
                dve.wait_ge(ph_ready, i + 1)
                dve.tensor_tensor(mix_lo[:, ds(i), :], pool_f[:], mix_hi[:, ds(i), :].bitcast(F32),
                                  ALU.subtract).then_inc(pl_ready, 1)
                split_weight(SLOTS * i + 5, 1)
                dve.wait_ge(c_copied, i + 1)
                dve.sem_inc(bank_free[1], 1)
                dve.wait_ge(job_done, SLOTS * i + 3)
                chain.did(dve.tensor_tensor(z_pad[:, TAPS - 1:], bank[2][:], c_sb[:], ALU.mult))
                split_weight(SLOTS * i + 6, 2)
                chain.wait()
                dve.sem_inc(bank_free[2], 1)
                chain.did(dve.tensor_scalar(conv[:, 0, :], z_pad[:, 0:T], tap(0), None, ALU.mult))
                chain.wait()
                chain.did(dve.scalar_tensor_tensor(conv[:, 1, :], z_pad[:, 1:1 + T], tap(1), conv[:, 0, :],
                                                   ALU.mult, ALU.add))
                chain.wait()
                chain.did(dve.scalar_tensor_tensor(conv[:, 0, :], z_pad[:, 2:2 + T], tap(2), conv[:, 1, :],
                                                   ALU.mult, ALU.add))
                dve.wait_ge(job_done, SLOTS * i + 4)
                chain.wait()
                dve.tensor_tensor(u_f[:], bank[3][:], conv[:, 0, :], ALU.mult).then_inc(uf_ready, 1)
                split_weight(SLOTS * i + 7, 3)
                dve.wait_ge(uh_ready, i + 1)
                dve.sem_inc(bank_free[3], 1)
                dve.tensor_tensor(u_lo[:, ds(i), :], u_f[:], u_hi[:, ds(i), :].bitcast(F32), ALU.subtract
                                  ).then_inc(ul_ready, 1)

            for g, window in enumerate(WINDOWS):
                with dve.Fori(2 * g, 2 * g + 2) as i:
                    chain.enter(i - 2 * g, 4 + (window.bit_length() - 1) + 2)
                    in_block(i, window)
                chain.leave(2)

            for g in range(N_POOL):
                for jo in range(2):
                    j = 2 * g + jo
                    dve.wait_ge(mh_ready, j + 1)
                    dve.tensor_tensor(mix_lo[:, j, :], mixed_f[:], mix_hi[:, j, :].bitcast(F32), ALU.subtract
                                      ).then_inc(ml_ready, 1)
                split_weight(AT_GATE + g, g)

            with dve.Fori(0, NB) as i:
                chain.enter(i, 2)
                for b in range(2):
                    dve.wait_ge(sigmoids, 2 * i + (b + 1))
                    dve.sem_inc(bank_free[b], 1)
                    split_weight(SLOTS * i + (AT_GATE + SLOTS + b), b)
                for b, sig in ((2, sig_a), (3, sig_b)):
                    dve.wait_ge(job_done, SLOTS * i + (AT_GATE + b + 1))
                    chain.did(dve.tensor_tensor(sig[:], bank[b][:], sig[:], ALU.mult))
                    split_weight(SLOTS * i + (AT_GATE + SLOTS + b), b)
                    chain.wait()
                    dve.sem_inc(bank_free[b], 1)
                dve.tensor_tensor(scratch[:, 0, :], sig_a[:], sig_b[:], ALU.add).then_inc(gf_ready, 1)
                dve.wait_ge(gh_ready, i + 1)
                dve.tensor_tensor(merged_lo[:, ds(i), :], scratch[:, 0, :], merged_hi[:, ds(i), :].bitcast(F32),
                                  ALU.subtract).then_inc(gl_ready, 1)
            chain.leave(NB)

            chain.did(dve.memset(row_stat[:], 0.0))
            with dve.Fori(0, NB // SLOTS) as i:
                chain.enter(i, SLOTS)
                for b in range(SLOTS):
                    block_j = h_t[:, ds(SLOTS * i + b), :].rearrange("p o t -> p (o t)")
                    dve.wait_ge(job_done, SLOTS * i + (AT_OUT + b + 1))
                    dve.tensor_tensor(block_j, bank[b][:], block_j, ALU.add).then_inc(h_ready, 1)
                    split_weight(SLOTS * i + (AT_OUT + SLOTS + b), b)
                    dve.wait_ge(squared, SLOTS * i + (NB + b + 1))
                    dve.sem_inc(bank_free[b], 1)
                    chain.wait()
                    chain.did(dve.tensor_tensor(row_stat[:], row_stat[:], scratch[:, b % 2, :], ALU.add))
            chain.leave(NB // SLOTS)
            chain.wait()
            dve.sem_inc(h_ready, 1)
            dve.wait_ge(summed, 2)
            inverse_rms(bank[4], 1)
            norm_apply(NB, COL_G_FFN)

            def u_split(step, b):
                dve.wait_ge(act_ready, SLOTS * step + (b + 1))
                dve.sem_inc(bank_free[b], 1)
                split_weight(SLOTS * step + (AT_U + SLOTS + b), b)

            def retrieve(h, c, split):
                halves = [(k, k // 2, k % 2) for k in range(4)]
                row = lambda k: keyed[:, k, :]
                chain.did(dve.tensor_copy(keyed[:].rearrange("p (u h) n -> p u h n", u=2),
                                          scores[:, c:c + 2, ds(2 * h, 2), :]))
                chain.hold(held)
                for k, u, half in halves:
                    chain.did(dve.max(top_v[:, half, u, 0:8], row(k)))
                chain.hold(held)
                for k, u, half in halves:
                    chain.did(dve.max_index(top_i[:, half, u, 0:8], top_v[:, half, u, 0:8], row(k)))
                    chain.did(dve.match_replace(less[:, k, :], top_v[:, half, u, 0:8], row(k), LOWEST))
                split(0)
                chain.hold(held)
                for k, u, half in halves:
                    chain.did(dve.max(top_v[:, half, u, 8:16], less[:, k, :]))
                chain.hold(held)
                for k, u, half in halves:
                    chain.did(dve.max_index(top_i[:, half, u, 8:16], top_v[:, half, u, 8:16], less[:, k, :]))
                shape = [P, 2, TOPK, TOPK]
                for first, count, width, at in ((0, TOP_A, TOPK, 0), (TOP_A, TOPK - TOP_A, LOW_B, WIDE)):
                    part = [P, 2, count, width]
                    chain.did(dve.tensor_tensor(
                        cand[:, :, at:at + count * width].rearrange("p u (a b) -> p u a b", a=count),
                        top_v[:, 0, :, first:first + count].unsqueeze(3).broadcast_to(part),
                        top_v[:, 1, :, 0:width].unsqueeze(2).broadcast_to(part), ALU.add))
                split(1)
                chain.hold(held)
                unit = lambda u: top_c[:, u, :]
                for u in range(2):
                    chain.did(dve.max(unit(u)[:, 0:8], cand[:, u, :]))
                chain.hold(held)
                for u in range(2):
                    chain.did(dve.max_index(pos[:, u, 0:8], unit(u)[:, 0:8], cand[:, u, :]))
                    chain.did(dve.match_replace(cand_less[:, u, :], unit(u)[:, 0:8], cand[:, u, :], LOWEST))
                chain.hold(held)
                for u in range(2):
                    chain.did(dve.max(unit(u)[:, 8:16], cand_less[:, u, :]))
                split(2)
                chain.hold(held)
                for u in range(2):
                    chain.did(dve.max_index(pos[:, u, 8:16], unit(u)[:, 8:16], cand_less[:, u, :]))
                chain.wait()
                chain.did(dve.tensor_copy(best[:, c:c + 2, ds(h), :], top_c[:].unsqueeze(2)))
                wide_a, low_a, low_b, high_b = (parts[:, k, :, :] for k in range(4))
                chain.did(dve.tensor_single_scalar(wide_a, pos[:], 4, ALU.logical_shift_right))
                chain.did(dve.tensor_single_scalar(low_a, pos[:], 2, ALU.logical_shift_right))
                chain.did(dve.tensor_single_scalar(low_b, pos[:], LOW_B - 1, ALU.bitwise_and))
                chain.did(dve.tensor_single_scalar(high_b, pos[:], TOPK - LOW_B, ALU.bitwise_and))
                chain.wait()
                chain.did(dve.scalar_tensor_tensor(rank[:, 0, :, :], low_a, float(TOP_A - WIDE // LOW_B), wide_a,
                                                   ALU.add, ALU.max))
                chain.did(dve.scalar_tensor_tensor(high_b, pos[:], float(WIDE), high_b, ALU.is_lt, ALU.mult))
                chain.wait()
                chain.did(dve.scalar_tensor_tensor(rank[:, 1, :, :], low_b, 0.0, high_b, ALU.add, ALU.add))
                chain.wait()
                both = "p h u j r -> p (h u) j r"
                shape = [P, 4, TOPK, TOPK]
                chain.did(dve.tensor_tensor(
                    found[:].rearrange(both),
                    rank[:].rearrange("p h u r -> p (h u) r").unsqueeze(2).broadcast_to(shape),
                    iota_place[:].unsqueeze(1).broadcast_to(shape), ALU.is_equal))
                split(3)
                chain.wait()
                chain.did(dve.tensor_tensor(
                    found[:].rearrange(both), found[:].rearrange(both),
                    top_i[:].rearrange("p h u j -> p (h u) j").unsqueeze(3).broadcast_to(shape), ALU.mult))
                chain.wait()
                for half, to in enumerate((e1, e2)):
                    chain.did(dve.tensor_reduce(to[:, c:c + 2, ds(h), :].rearrange("p c o r -> p c (o r)"),
                                                found[:, half].rearrange("p u j r -> p u r j"), AX.X, ALU.add))

            def q_split(i, b):
                dve.wait_ge(q_ready, SLOTS * i + b + 1)
                dve.sem_inc(bank_free[b], 1)
                split_weight(AT_QUERY + SLOTS * (i + 1) + b, b)

            for b in range(SLOTS):
                q_split(0, b)
            for i, (h, c) in enumerate(((0, 0), (0, 2), (1, 0)), 1):
                dve.wait_ge(scores_ready, SLOTS)
                retrieve(h, c, lambda b: q_split(i, b))
            retrieve(1, 2, lambda b: u_split(0, b))
            dve.wait_ge(scores_ready, HALVES)
            with dve.Fori(2, HEADS - 1) as h:
                chain.enter(h - 2, 2 * 45)
                for k in range(2):
                    retrieve(h, 2 * k, lambda b: u_split(2 * h + (k - 3), b))
            chain.leave(HEADS - 3)
            retrieve(HEADS - 1, 0, lambda b: u_split(TOPK_STEPS - 2, b))
            chain.wait()

            flat = lambda tensor: tensor[:, 0, :, :].rearrange("p h r -> p (h r)")
            for k in range(2):
                chain.did(dve.scalar_tensor_tensor(expert[:, k * PAIRS:(k + 1) * PAIRS], flat(e2), float(KEYS),
                                                   flat(e1), ALU.mult, ALU.add))
            chain.wait()
            chain.did(dve.tensor_copy(expert[:, 2 * PAIRS:], expert[:, 0:ROW_SLOTS]))
            chain.did(dve.tensor_copy(row_index[:], expert[:, 0:ROW_SLOTS]))
            chain.wait()
            dve.sem_inc(rows_used, ROW_SLOTS)
            retrieve(HEADS - 1, 2, lambda b: u_split(TOPK_STEPS - 1, b))
            chain.wait()

            over_ranks = lambda tensor: tensor[:].unsqueeze(3).broadcast_to([P, CHUNKS, HEADS, TOPK])
            chain.did(dve.tensor_copy(denom[:].unsqueeze(3), best[:, :, :, 0:1]))
            chain.wait()
            dve.tensor_tensor(best[:], best[:], over_ranks(denom), ALU.subtract).then_inc(shifted, 1)

            def use_row(r, slot, times, use):
                dve.wait_ge(rows_loaded[slot], 16 * times)
                dve.tensor_copy(row_index[:, slot:slot + 1], expert[:, ds(r + ROW_SLOTS)])
                use(r, slot).then_inc(rows_used, 1)

            def dot(r, slot):
                return dve.scalar_tensor_tensor(rows[:, slot, :], rows[:, slot, :], 1.0, x_tok[:], ALU.mult, ALU.mult,
                                                accum_out=dots[:, ds(r)])

            def u_dots(s, per_pass, at, first, count):
                for k in range(first, first + count):
                    use_row(per_pass * s + (at + k), k % ROW_SLOTS,
                            per_pass // ROW_SLOTS * s + (at // ROW_SLOTS + k // ROW_SLOTS + 1), dot)

            dve.wait_ge(x_tok_ready, 2)
            for b in range(SLOTS - 1):
                u_split(TOPK_STEPS, b)
                u_dots(0, 8, 0, 2 * b, 2)
            dve.wait_ge(exp_ready, 1)
            chain.did(dve.tensor_reduce(denom[:], best[:], AX.X, ALU.add))
            chain.wait()
            chain.did(dve.reciprocal(denom[:], denom[:]))
            chain.wait()
            dve.tensor_tensor(best[:], best[:], over_ranks(denom), ALU.mult).then_inc(gates_ready, 1)
            u_split(TOPK_STEPS, SLOTS - 1)
            u_dots(0, 8, 0, 2 * (SLOTS - 1), 2)

            def gates_at_keys(s, q):
                if q >= GROUPS_PER_ROUND:
                    s, q = s + 1, q - GROUPS_PER_ROUND
                dve.wait_ge(onehots_used, GROUPS_PER_ROUND * s + (q + 1))
                for t in range(TOKENS_PER_GROUP):
                    token = ds(TOKENS_PER_ROUND * s + (TOKENS_PER_GROUP * q + t))
                    if q % 4 == 3:
                        dve.tensor_scalar(oh1[:, q % SLOTS, t, :], iota_key[:], e1_t[:, token], None,
                                          ALU.is_equal)
                    last = dve.tensor_scalar(oh2[:, q % SLOTS, t, :], iota_key[:], e2_t[:, token],
                                             gate_t[:, token], ALU.is_equal, ALU.mult)
                last.then_inc(oh2_ready, 1)

            def dve_round(s, last=False):
                for b in range(ROUND * SLOTS):
                    for q in (2 * b + 2, 2 * b + 3):
                        if not last or q < GROUPS_PER_ROUND:
                            gates_at_keys(s, q)
                    u_split(ROUND * s + (ONEHOT_AT + b // SLOTS), b % SLOTS)
                    u_dots(s, sum(ROWS_OF_ROUND), ROWS_ONEHOT, sum(ROWS_OF_ROUND[:b]), ROWS_OF_ROUND[b])

            for b in range(SLOTS):
                u_split(TOPK_STEPS + 1, b)
                if b == 2:
                    dve.wait_ge(turned_copied, 3)
                    for q in range(2):
                        gates_at_keys(0, q)
                u_dots(0, 8, 8, 2 * b, 2)

            with dve.Fori(0, ROUNDS - 1) as s:
                dve_round(s)
            dve_round(ROUNDS - 1, last=True)
            with dve.Fori(0, U_STEPS - 1 - PLAIN_AT) as s:
                for b in range(SLOTS):
                    u_split(s + PLAIN_AT, b)
                    u_dots(s, 8, ROWS_PLAIN, 2 * b, 2)

            def mask(g, b, parity):
                m = SLOTS * g + b
                if isinstance(g, int) and g < KEPT_STEPS:
                    dve.wait_ge(act_ready, SLOTS * (U_STEPS - KEPT_STEPS + g) + b + 1)
                    source = kept_at(g, b)
                else:
                    dve.wait_ge(act_loaded[b], 16 * g + (16 - 16 * KEPT_STEPS))
                    source = act_in[:, b, :]
                if b == 0:
                    dve.wait_ge(g_loaded, 16 * g + 16)
                if b >= 2 or not isinstance(g, int) or g > 0:
                    dve.wait_ge(al_ready, m - 1)
                dve.tensor_tensor(a_f[:, b % 2, :].rearrange("p (c t) -> p c t", t=PIECE),
                                  source.rearrange("p (c t) -> p c t", t=PIECE),
                                  g_in[parity][:, :, b, :], ALU.mult).then_inc(af_ready, 1)

            def mask_lo(m, b):
                dve.wait_ge(ah_ready, m + 1)
                dve.tensor_tensor(a_lo[:, b, :], a_f[:, b % 2, :], a_hi[:, b, :].bitcast(F32), ALU.subtract
                                  ).then_inc(al_ready, 1)

            for b in range(SLOTS):
                mask(0, b, 0)
                u_split(U_STEPS - 1, b)
                mask_lo(b, b)

            def accumulate(r, slot):
                return dve.scalar_tensor_tensor(out_tok[:], rows[:, slot, :], dots[:, ds(r - PAIRS)], out_tok[:],
                                                ALU.mult, ALU.add)

            def v_row(i, slot, times):
                dve.wait_ge(rows_used, i + (ROW_SLOTS + PAIRS))
                use_row(i + PAIRS, slot, times, accumulate)

            def v_split(g, b, parity):
                mask(g, b, parity)
                split_weight(SLOTS * g + (AT_V + b), b)
                mask_lo(SLOTS * g + b, b)

            for b in range(SLOTS):
                v_split(1, b, 1)
                u_dots(0, 8, PAIRS - 8, 2 * b, 2)
            for g in range(2, KEPT_STEPS + 1):
                for b in range(SLOTS):
                    v_split(g, b, g % 2)
                    if (g, b) == (2, 0):
                        chain.did(dve.memset(out_tok[:], 0.0))
                        dve.wait_ge(dots_gelu, 1)
                        chain.did(dve.tensor_tensor(dots[:], dots[:], flat(best), ALU.mult))
                        chain.wait()
                    for i in range((SLOTS + 1) * (g - 2) + b, (SLOTS + 1) * (g - 2) + b + 1 + (b == SLOTS - 1)):
                        v_row(i, i % ROW_SLOTS, (PAIRS + i) // ROW_SLOTS + 1)
            with dve.Fori((KEPT_STEPS + 1) // 2, U_STEPS // 2) as i:
                for k in range(2):
                    for b in range(SLOTS):
                        v_split(2 * i + k, b, k)
                        v_row(SLOTS * (2 * i + k) + (b - SLOTS), b, 2 * i + (k + PAIRS // ROW_SLOTS))
            for b in range(SLOTS):
                v_row(PAIRS - SLOTS + b, b, 2 * PAIRS // ROW_SLOTS)
            dve.wait_ge(rows_used, ROW_SLOTS + 2 * PAIRS)
            dve.sem_inc(tok_done, 1)

            def add_pair(j):
                dve.wait_ge(squared, 2 * NB + 2 * j + 2)
                dve.tensor_tensor(squares[:, 2 * j, :], squares[:, 2 * j, :], squares[:, 2 * j + 1, :],
                                  ALU.add).then_inc(added, 1)

            for j in range(NB):
                dve.wait_ge(acc_done, j + 1)
                dve.tensor_tensor(h_t[:, j, :], bank[j][:], h_t[:, j, :], ALU.add).then_inc(h2_ready, 1)
                if j >= 3 and j % 2 == 1:
                    add_pair((j - 3) // 2)
            add_pair(NB // 2 - 1)
            dve.wait_ge(summed, 2 + NB // 2)
            inverse_rms(bank[0], NB // 2)
            for j in range(NB):
                dve.scalar_tensor_tensor(out_sb[:, j, :], h_t[:, j, :],
                                         params[:, COL_G_FIN + j:COL_G_FIN + j + 1], bank[1][:],
                                         ALU.mult, ALU.mult).then_inc(out_ready, 1)


def tiles(w):
    return w.reshape(NB, P, -1, P).transpose(2, 1, 0, 3).reshape(-1, P, D)


def per_channel(v):
    return v.reshape(NB, P).T


def kernel(x, norm_mix_g, w_in, conv_w, w_conv_out, pool_w, pool_scale, w_pool_out, w_out, norm_ffn_g,
           w_query, sub_keys, expert_u, expert_v, norm_final_g):
    import concourse.bacc as bacc
    from concourse.bass_utils import run_bass_kernel_spmd

    a = {k: np.asarray(v) for k, v in locals().items() if k not in ("bacc", "run_bass_kernel_spmd")}
    w = tiles(a["w_in"][0]).reshape(6, NB, P, D)
    by_block = lambda *parts: np.stack(parts, 1).reshape(-1, P, D)
    inv_count = np.broadcast_to(1.0 / np.arange(1, PAD + 1, dtype=np.float32), (P, PAD)).astype(np.float32)
    conv_cols = a["conv_w"][0].reshape(TAPS, NB, P).transpose(2, 1, 0).reshape(P, NB * TAPS)
    pool_tiles = a["pool_w"][0].reshape(N_POOL, 2, P, 2 * P).transpose(0, 2, 1, 3).reshape(N_POOL, P, 4 * P)
    arrays = {
        "x_t": a["x"][0].T.reshape(NB, P, T).transpose(1, 0, 2),
        "params": np.concatenate([per_channel(a["norm_mix_g"][0]), per_channel(a["norm_ffn_g"][0]),
                                  per_channel(a["norm_final_g"]), per_channel(a["pool_scale"][0]),
                                  conv_cols, inv_count], 1),
        "w_in": by_block(w[3], w[1], w[2], w[0]),
        "pool": np.concatenate([pool_tiles, np.zeros_like(pool_tiles)], 2),
        "gate": by_block(w[4], w[5], tiles(a["w_conv_out"][0]), tiles(a["w_pool_out"][0])),
        "w_out": tiles(a["w_out"][0]),
        "query": tiles(a["w_query"][0]),
        "keys": a["sub_keys"][0].transpose(3, 0, 1, 2).reshape(P, HALVES, KEYS),
        "u": a["expert_u"][0].reshape(KEYS, KEYS, NB, P).transpose(1, 3, 2, 0).reshape(KEYS, P, D),
        "v": a["expert_v"][0].reshape(KEYS, KEYS, D).transpose(1, 0, 2),
        "u_rows": a["expert_u"][0].reshape(KEYS, KEYS, D).transpose(1, 0, 2),
    }
    arrays = {k: np.ascontiguousarray(v) for k, v in arrays.items()}
    nc = bacc.Bacc("TRN2", target_bir_lowering=False, num_devices=1)
    aps = [nc.dram_tensor(k, v.shape, F32, kind="ExternalInput").ap() for k, v in arrays.items()]
    out = nc.dram_tensor("out", (P, NB, T), F32, kind="ExternalOutput").ap()
    act_dram = nc.dram_tensor("act_dram", (KEYS, P, DT), F32, kind="Internal").ap()
    g_dram = nc.dram_tensor("g_dram", (P, N_PIECES, KEYS, PIECE), F32, kind="Internal").ap()
    build(nc, *aps, out, act_dram, g_dram)
    got = run_bass_kernel_spmd(nc, [arrays], core_ids=[0]).results[0]["out"]
    return np.ascontiguousarray(got.transpose(1, 0, 2).reshape(D, T).T).reshape(1, T, D)
```
